# Optimizing a Trainium2 kernel written in Bass

```python
import math
import jax, jax.numpy as jnp
from jax import lax
import numpy as np

D_MODEL = 1024
BATCH = 1
SEQ = 512
DEPTH = 1

GDN_HEADS = 8
GDN_DK = 128
GDN_DV = 128
GDN_CONV = 4
GDN_CHUNK = 64
DSA_HEADS = 8
DSA_KV_HEADS = 2
DSA_DH = 128
IDX_HEADS = 8
IDX_DIM = 64
TOPK_MAX = 256
Q_BLOCK = 128
D_FF = 2816
FFN_CONV = 3
EPS = 1e-6

GDN_QK_W = GDN_HEADS * GDN_DK
GDN_V_W = GDN_HEADS * GDN_DV
GDN_CONV_CH = 2 * GDN_QK_W + GDN_V_W
DSA_Q_W = DSA_HEADS * DSA_DH
DSA_KV_W = DSA_KV_HEADS * DSA_DH
IDX_Q_W = IDX_HEADS * IDX_DIM
IN_SPLITS = (GDN_CONV_CH, GDN_V_W, GDN_HEADS, GDN_HEADS,
             DSA_Q_W, DSA_KV_W, DSA_KV_W, IDX_Q_W, IDX_DIM, IDX_HEADS,
             D_MODEL, D_MODEL)
N_IN = GDN_CONV_CH + GDN_V_W + 2 * GDN_HEADS + DSA_Q_W + 2 * DSA_KV_W + IDX_Q_W + IDX_DIM + IDX_HEADS + 2 * D_MODEL


def rmsnorm(x, g):
    xf = x.astype(jnp.float32)
    y = xf * lax.rsqrt(jnp.mean(xf * xf, axis=-1, keepdims=True) + EPS)
    return (y * g.astype(jnp.float32)).astype(x.dtype)

def layernorm_nobias(x, g):
    xf = x.astype(jnp.float32)
    xc = xf - jnp.mean(xf, axis=-1, keepdims=True)
    y = xc * lax.rsqrt(jnp.mean(xc * xc, axis=-1, keepdims=True) + EPS)
    return (y * g.astype(jnp.float32)).astype(x.dtype)

def l2norm(x):
    xf = x.astype(jnp.float32)
    return xf * lax.rsqrt(jnp.sum(xf * xf, axis=-1, keepdims=True) + EPS)

def causal_dwconv(x, w):
    width, ch = w.shape
    return lax.conv_general_dilated(
        x, w[:, None, :].astype(x.dtype), window_strides=(1,),
        padding=[(width - 1, 0)], dimension_numbers=("NWC", "WIO", "NWC"),
        feature_group_count=ch)

def gated_delta_rule_chunked(q, k, v, g, beta):
    B, S, H, dk = q.shape
    dv = v.shape[-1]
    C = GDN_CHUNK
    N = S // C
    q = q * (dk ** -0.5)

    def chunks(t):
        return jnp.swapaxes(t.reshape((B, N, C) + t.shape[2:]), 2, 3)

    qc, kc, vc, gc, bc = chunks(q), chunks(k), chunks(v), chunks(g), chunks(beta)
    G = jnp.cumsum(gc, axis=-1)
    tri = jnp.tril(jnp.ones((C, C), dtype=bool))
    strict = jnp.tril(jnp.ones((C, C), dtype=bool), -1)
    gamma = jnp.exp(jnp.where(tri, G[..., :, None] - G[..., None, :], -jnp.inf))
    kb = kc * bc[..., None]
    A = jnp.where(strict, jnp.einsum("bnhid,bnhjd->bnhij", kb, kc) * gamma, 0.0)
    eye = jnp.eye(C, dtype=jnp.float32)
    T = lax.linalg.triangular_solve(A + eye, jnp.broadcast_to(eye, A.shape),
                                    left_side=True, lower=True)
    eG = jnp.exp(G)[..., None]
    u = jnp.einsum("bnhij,bnhje->bnhie", T, vc * bc[..., None])
    w = jnp.einsum("bnhij,bnhjd->bnhid", T, kb * eG)
    qg = qc * eG
    kd = kc * jnp.exp(G[..., -1:] - G)[..., None]
    att = jnp.einsum("bnhid,bnhjd->bnhij", qc, kc) * gamma
    dlast = jnp.exp(G[..., -1])

    def step(state, inp):
        u_i, w_i, qg_i, kd_i, att_i, dl_i = inp
        v_new = u_i - jnp.einsum("bhcd,bhde->bhce", w_i, state)
        o = jnp.einsum("bhcd,bhde->bhce", qg_i, state) + jnp.einsum("bhij,bhje->bhie", att_i, v_new)
        state = state * dl_i[..., None, None] + jnp.einsum("bhcd,bhce->bhde", kd_i, v_new)
        return state, o

    xs = (jnp.swapaxes(u, 0, 1), jnp.swapaxes(w, 0, 1), jnp.swapaxes(qg, 0, 1),
          jnp.swapaxes(kd, 0, 1), jnp.swapaxes(att, 0, 1), jnp.swapaxes(dlast, 0, 1))
    s0 = jnp.zeros((B, H, dk, dv), jnp.float32)
    _, o = lax.scan(step, s0, xs)
    return jnp.transpose(o, (1, 0, 3, 2, 4)).reshape(B, S, H, dv)

def dsa_sparse_attention(q, k, v, iq, ik, iw):
    B, S, Hq, dh = q.shape
    L, Hkv = k.shape[1], k.shape[2]
    k_top = min(TOPK_MAX, L // 4)
    rep = Hq // Hkv
    nb = S // Q_BLOCK
    key_pos = jnp.arange(L, dtype=jnp.int32)
    starts = jnp.arange(nb, dtype=jnp.int32) * Q_BLOCK
    iw = iw * ((IDX_HEADS ** -0.5) * (IDX_DIM ** -0.5))

    def blocks(t):
        return jnp.swapaxes(t.reshape((B, nb, Q_BLOCK) + t.shape[2:]), 0, 1)

    def one_block(args):
        q_b, iq_b, iw_b, start = args
        t_pos = start + jnp.arange(Q_BLOCK, dtype=jnp.int32)
        causal = key_pos[None, :] <= t_pos[:, None]
        rel = jax.nn.relu(jnp.einsum("bqhd,bsd->bqhs", iq_b, ik))
        score = jnp.einsum("bqh,bqhs->bqs", iw_b, rel).astype(jnp.float32)
        score = jnp.where(causal[None], score, -jnp.inf)
        _, idx = lax.top_k(score, k_top)
        valid = idx <= t_pos[None, :, None]
        k_sel = jax.vmap(lambda kb, ib: kb[ib])(k, idx)
        v_sel = jax.vmap(lambda vb, ib: vb[ib])(v, idx)
        qg = q_b.reshape(B, Q_BLOCK, Hkv, rep, dh)
        logits = jnp.einsum("bqgrd,bqkgd->bqgrk", qg, k_sel).astype(jnp.float32) * (dh ** -0.5)
        logits = jnp.where(valid[:, :, None, None, :], logits, -jnp.inf)
        p = jax.nn.softmax(logits, axis=-1).astype(v.dtype)
        o = jnp.einsum("bqgrk,bqkgd->bqgrd", p, v_sel)
        return o.reshape(B, Q_BLOCK, Hq * dh)

    out = lax.map(one_block, (blocks(q), blocks(iq), blocks(iw), starts))
    return jnp.swapaxes(out, 0, 1).reshape(B, S, Hq * dh)

def first_inputs(seed: int = 0) -> dict:
    key = jax.random.key(seed)
    ks = jax.random.split(key, 16)
    f32 = jnp.float32

    def nrm(k, shape, scale):
        return jax.random.normal(k, shape, f32) * scale

    x = nrm(ks[0], (BATCH, SEQ, D_MODEL), 1.0)
    norm1_g = 1.0 + nrm(ks[1], (DEPTH, D_MODEL), 0.02)
    w_in = nrm(ks[2], (DEPTH, D_MODEL, N_IN), D_MODEL ** -0.5)
    gdn_conv_w = nrm(ks[3], (DEPTH, GDN_CONV, GDN_CONV_CH), GDN_CONV ** -0.5)
    gdn_a_log = jnp.log(jax.random.uniform(ks[4], (DEPTH, GDN_HEADS), f32, 1.0, 16.0))
    dt = jnp.exp(jax.random.uniform(ks[5], (DEPTH, GDN_HEADS), f32, math.log(1e-3), math.log(1e-1)))
    gdn_dt_bias = dt + jnp.log(-jnp.expm1(-dt))
    gdn_norm_g = 1.0 + nrm(ks[6], (DEPTH, GDN_DV), 0.02)
    idx_k_norm_g = 1.0 + nrm(ks[7], (DEPTH, IDX_DIM), 0.02)
    branch_gate_b = nrm(ks[8], (DEPTH, 2 * D_MODEL), 0.02)
    w_out = nrm(ks[9], (DEPTH, D_MODEL, D_MODEL), D_MODEL ** -0.5)
    norm2_g = 1.0 + nrm(ks[10], (DEPTH, D_MODEL), 0.02)
    ffn_w_up = nrm(ks[11], (DEPTH, D_MODEL, 2 * D_FF), D_MODEL ** -0.5)
    ffn_conv_w = nrm(ks[12], (DEPTH, FFN_CONV, 2 * D_FF), FFN_CONV ** -0.5)
    ffn_conv_b = nrm(ks[13], (DEPTH, 2 * D_FF), 0.02)
    ffn_w_down = nrm(ks[14], (DEPTH, D_FF, D_MODEL), D_FF ** -0.5)
    final_g = 1.0 + nrm(ks[15], (D_MODEL,), 0.02)
    return {"x": x, "norm1_g": norm1_g, "w_in": w_in, "gdn_conv_w": gdn_conv_w,
            "gdn_a_log": gdn_a_log, "gdn_dt_bias": gdn_dt_bias, "gdn_norm_g": gdn_norm_g,
            "idx_k_norm_g": idx_k_norm_g, "branch_gate_b": branch_gate_b, "w_out": w_out,
            "norm2_g": norm2_g, "ffn_w_up": ffn_w_up, "ffn_conv_w": ffn_conv_w,
            "ffn_conv_b": ffn_conv_b, "ffn_w_down": ffn_w_down, "final_g": final_g}

def first_block(x, norm1_g, w_in, gdn_conv_w, gdn_a_log, gdn_dt_bias, gdn_norm_g,
              idx_k_norm_g, branch_gate_b, w_out, norm2_g, ffn_w_up, ffn_conv_w,
              ffn_conv_b, ffn_w_down, final_g):
    B, S, _ = x.shape
    offsets = [int(o) for o in np.cumsum(IN_SPLITS)[:-1]]
    h = x
    for l in range(DEPTH):
        u = rmsnorm(h, norm1_g[l])
        proj = jnp.einsum("bsd,de->bse", u, w_in[l])
        (g_qkv, g_z, g_a, g_b, d_q, d_k, d_v, i_q, i_k, i_w, gate_a, gate_b) = jnp.split(proj, offsets, axis=-1)

        qkv = jax.nn.silu(causal_dwconv(g_qkv, gdn_conv_w[l]))
        gq, gk, gv = jnp.split(qkv, [GDN_QK_W, 2 * GDN_QK_W], axis=-1)
        gq = l2norm(gq.reshape(B, S, GDN_HEADS, GDN_DK))
        gk = l2norm(gk.reshape(B, S, GDN_HEADS, GDN_DK))
        gv = gv.reshape(B, S, GDN_HEADS, GDN_DV).astype(jnp.float32)
        beta = jax.nn.sigmoid(g_b.astype(jnp.float32))
        logdecay = -jnp.exp(gdn_a_log[l].astype(jnp.float32)) * jax.nn.softplus(
            g_a.astype(jnp.float32) + gdn_dt_bias[l].astype(jnp.float32))
        o_gdn = gated_delta_rule_chunked(gq, gk, gv, logdecay, beta)
        z = g_z.reshape(B, S, GDN_HEADS, GDN_DV).astype(jnp.float32)
        o_gdn = (rmsnorm(o_gdn, gdn_norm_g[l]) * jax.nn.silu(z)).reshape(B, S, GDN_V_W).astype(x.dtype)

        o_dsa = dsa_sparse_attention(
            d_q.reshape(B, S, DSA_HEADS, DSA_DH),
            d_k.reshape(B, S, DSA_KV_HEADS, DSA_DH),
            d_v.reshape(B, S, DSA_KV_HEADS, DSA_DH),
            i_q.reshape(B, S, IDX_HEADS, IDX_DIM),
            layernorm_nobias(i_k, idx_k_norm_g[l]),
            i_w)

        gb = branch_gate_b[l]
        mixed = (jax.nn.sigmoid(gate_a + gb[:D_MODEL]) * o_gdn
                 + jax.nn.sigmoid(gate_b + gb[D_MODEL:]) * o_dsa)
        h = h + jnp.einsum("bse,ed->bsd", mixed, w_out[l])

        hn = rmsnorm(h, norm2_g[l])
        up = causal_dwconv(jnp.einsum("bsd,df->bsf", hn, ffn_w_up[l]), ffn_conv_w[l]) + ffn_conv_b[l]
        f_gate, f_val = jnp.split(up, [D_FF], axis=-1)
        h = h + jnp.einsum("bsf,fd->bsd", jax.nn.silu(f_gate) * f_val, ffn_w_down[l])
    return rmsnorm(h, final_g)


DEPTH_2 = 2

N_A = DEPTH_2 // 2
N_B = DEPTH_2 - N_A
RMS_EPS = 1e-6

FOX_HEADS = 16
FOX_HEAD_DIM = D_MODEL // FOX_HEADS
FOX_WIDTH = FOX_HEADS * FOX_HEAD_DIM

MLA_HEADS = 16
MLA_NOPE = 64
MLA_ROPE = 32
MLA_V = 64
KV_RANK = 4 * MLA_V
Q_RANK = 12 * MLA_V
ROPE_THETA = 10000.0

D_FF_2 = ((8 * D_MODEL // 3 + 255) // 256) * 256


def rmsnorm_2(x, g):
    xf = x.astype(jnp.float32)
    inv = lax.rsqrt(jnp.mean(xf * xf, axis=-1, keepdims=True) + RMS_EPS)
    return (xf * inv).astype(x.dtype) * g

def rope(x, positions):
    d = x.shape[-1]
    inv_freq = ROPE_THETA ** (-jnp.arange(0, d // 2, dtype=jnp.float32) * 2.0 / d)
    ang = positions.astype(jnp.float32)[..., None] * inv_freq
    cos = jnp.cos(ang)[:, :, None, :]
    sin = jnp.sin(ang)[:, :, None, :]
    xf = x.astype(jnp.float32)
    x1, x2 = xf[..., : d // 2], xf[..., d // 2:]
    out = jnp.concatenate([x1 * cos - x2 * sin, x1 * sin + x2 * cos], axis=-1)
    return out.astype(x.dtype)

def causal_block_attention(q, k, v, scale, log_f_cum=None):
    B, S, H, dq = q.shape
    nb = S // Q_BLOCK
    qb = q.reshape(B, nb, Q_BLOCK, H, dq).transpose(1, 0, 2, 3, 4)
    k_pos = jnp.arange(S)
    if log_f_cum is not None:
        cq_blocks = log_f_cum.reshape(B, nb, Q_BLOCK, H).transpose(1, 0, 2, 3)
        ck = log_f_cum.transpose(0, 2, 1)
    else:
        cq_blocks, ck = None, None

    def one_block(args):
        i, q_blk, cq = args
        s = jnp.einsum('bqhd,bkhd->bhqk', q_blk, k,
                       preferred_element_type=jnp.float32) * scale
        if cq is not None:
            s = s + (cq.transpose(0, 2, 1)[..., None] - ck[:, :, None, :])
        q_pos = i * Q_BLOCK + jnp.arange(Q_BLOCK)
        mask = k_pos[None, :] <= q_pos[:, None]
        s = jnp.where(mask[None, None], s, -jnp.inf)
        p = jax.nn.softmax(s, axis=-1)
        return jnp.einsum('bhqk,bkhd->bqhd', p.astype(v.dtype), v)

    out = lax.map(one_block, (jnp.arange(nb), qb, cq_blocks))
    return out.transpose(1, 0, 2, 3, 4).reshape(B, S, H, v.shape[-1])

def fox_attention(xn, w_in, b_f, w_o):
    B, S, _ = xn.shape
    proj = xn @ w_in
    q = proj[..., :FOX_WIDTH].reshape(B, S, FOX_HEADS, FOX_HEAD_DIM)
    k = proj[..., FOX_WIDTH:2 * FOX_WIDTH].reshape(B, S, FOX_HEADS, FOX_HEAD_DIM)
    v = proj[..., 2 * FOX_WIDTH:3 * FOX_WIDTH].reshape(B, S, FOX_HEADS, FOX_HEAD_DIM)
    f_logit = proj[..., 3 * FOX_WIDTH:] + b_f
    log_f = jax.nn.log_sigmoid(f_logit.astype(jnp.float32))
    cum = jnp.cumsum(log_f, axis=1)
    o = causal_block_attention(q, k, v, 1.0 / math.sqrt(FOX_HEAD_DIM), cum)
    return o.reshape(B, S, FOX_WIDTH) @ w_o

def mla_shared_kv(h, positions, kv_norm, w_kv_a, ckv_norm, w_uk, w_uv):
    B, S, _ = h.shape
    hn = rmsnorm_2(h, kv_norm)
    a = hn @ w_kv_a
    c_kv = rmsnorm_2(a[..., :KV_RANK], ckv_norm)
    k_rope = rope(a[..., KV_RANK:][:, :, None, :], positions)
    k_nope = jnp.einsum('bsr,rhd->bshd', c_kv, w_uk)
    v = jnp.einsum('bsr,rhd->bshd', c_kv, w_uv)
    k = jnp.concatenate(
        [k_nope, jnp.broadcast_to(k_rope, (B, S, MLA_HEADS, MLA_ROPE))], axis=-1)
    return k, v

def mla_attention(xn, positions, k, v, w_dq, cq_norm, w_uq, w_o):
    B, S, _ = xn.shape
    c_q = rmsnorm_2(xn @ w_dq, cq_norm)
    q = (c_q @ w_uq).reshape(B, S, MLA_HEADS, MLA_NOPE + MLA_ROPE)
    q = jnp.concatenate([q[..., :MLA_NOPE], rope(q[..., MLA_NOPE:], positions)], axis=-1)
    o = causal_block_attention(q, k, v, 1.0 / math.sqrt(MLA_NOPE + MLA_ROPE))
    return o.reshape(B, S, MLA_HEADS * MLA_V) @ w_o

def swiglu(xn, w_gate, w_up, w_down):
    return (jax.nn.silu(xn @ w_gate) * (xn @ w_up)) @ w_down

def second_inputs(seed: int = 0) -> dict:
    key = jax.random.key(seed)
    ks = jax.random.split(key, 24)

    def nrm(k, shape, fan_in):
        return jax.random.normal(k, shape, jnp.float32) * (fan_in ** -0.5)

    def gain(k, shape):
        return 1.0 + 0.02 * jax.random.normal(k, shape, jnp.float32)

    x = jax.random.normal(ks[0], (BATCH, SEQ, D_MODEL), jnp.float32)
    positions = jnp.broadcast_to(jnp.arange(SEQ, dtype=jnp.int32), (BATCH, SEQ))
    return {
        "x": x,
        "positions": positions,
        "attn_norm": gain(ks[1], (DEPTH_2, D_MODEL)),
        "ffn_norm": gain(ks[2], (DEPTH_2, D_MODEL)),
        "w_gate": nrm(ks[3], (DEPTH_2, D_MODEL, D_FF_2), D_MODEL),
        "w_up": nrm(ks[4], (DEPTH_2, D_MODEL, D_FF_2), D_MODEL),
        "w_down": nrm(ks[5], (DEPTH_2, D_FF_2, D_MODEL), D_FF_2),
        "fox_w_in": nrm(ks[6], (N_A, D_MODEL, 3 * FOX_WIDTH + FOX_HEADS), D_MODEL),
        "fox_b_f": 3.0 + 0.5 * jax.random.normal(ks[7], (N_A, FOX_HEADS), jnp.float32),
        "fox_w_o": nrm(ks[8], (N_A, FOX_WIDTH, D_MODEL), FOX_WIDTH),
        "kv_norm": gain(ks[9], (D_MODEL,)),
        "w_kv_a": nrm(ks[10], (D_MODEL, KV_RANK + MLA_ROPE), D_MODEL),
        "ckv_norm": gain(ks[11], (KV_RANK,)),
        "w_uk": nrm(ks[12], (KV_RANK, MLA_HEADS, MLA_NOPE), KV_RANK),
        "w_uv": nrm(ks[13], (KV_RANK, MLA_HEADS, MLA_V), KV_RANK),
        "mla_w_dq": nrm(ks[14], (N_B, D_MODEL, Q_RANK), D_MODEL),
        "cq_norm": gain(ks[15], (N_B, Q_RANK)),
        "mla_w_uq": nrm(ks[16], (N_B, Q_RANK, MLA_HEADS * (MLA_NOPE + MLA_ROPE)), Q_RANK),
        "mla_w_o": nrm(ks[17], (N_B, MLA_HEADS * MLA_V, D_MODEL), MLA_HEADS * MLA_V),
        "final_norm": gain(ks[18], (D_MODEL,)),
    }

def second_block(x, positions, attn_norm, ffn_norm, w_gate, w_up, w_down,
              fox_w_in, fox_b_f, fox_w_o, kv_norm, w_kv_a, ckv_norm, w_uk, w_uv,
              mla_w_dq, cq_norm, mla_w_uq, mla_w_o, final_norm):
    h = x
    k_shared, v_shared = None, None
    for l in range(DEPTH_2):
        if l == N_A:
            k_shared, v_shared = mla_shared_kv(h, positions, kv_norm, w_kv_a,
                                               ckv_norm, w_uk, w_uv)
        xn = rmsnorm_2(h, attn_norm[l])
        if l < N_A:
            h = h + fox_attention(xn, fox_w_in[l], fox_b_f[l], fox_w_o[l])
        else:
            j = l - N_A
            h = h + mla_attention(xn, positions, k_shared, v_shared,
                                  mla_w_dq[j], cq_norm[j], mla_w_uq[j], mla_w_o[j])
        h = h + swiglu(rmsnorm_2(h, ffn_norm[l]), w_gate[l], w_up[l], w_down[l])
    return rmsnorm_2(h, final_norm)


def setup_inputs(seed=0):
    out = dict(first_inputs(seed))
    for name, value in second_inputs(seed + 1).items():
        if name != "x":
            out[name + "_2"] = value
    return out


def reference(
    x, norm1_g, w_in, gdn_conv_w, gdn_a_log, gdn_dt_bias, gdn_norm_g, idx_k_norm_g,
    branch_gate_b, w_out, norm2_g, ffn_w_up, ffn_conv_w, ffn_conv_b, ffn_w_down, final_g,
    positions_2, attn_norm_2, ffn_norm_2, w_gate_2, w_up_2, w_down_2, fox_w_in_2, fox_b_f_2,
    fox_w_o_2, kv_norm_2, w_kv_a_2, ckv_norm_2, w_uk_2, w_uv_2, mla_w_dq_2, cq_norm_2,
    mla_w_uq_2, mla_w_o_2, final_norm_2,
):
    x = first_block(
        x, norm1_g, w_in, gdn_conv_w, gdn_a_log, gdn_dt_bias, gdn_norm_g, idx_k_norm_g,
        branch_gate_b, w_out, norm2_g, ffn_w_up, ffn_conv_w, ffn_conv_b, ffn_w_down, final_g,
    )
    return second_block(
        x, positions_2, attn_norm_2, ffn_norm_2, w_gate_2, w_up_2, w_down_2, fox_w_in_2,
        fox_b_f_2, fox_w_o_2, kv_norm_2, w_kv_a_2, ckv_norm_2, w_uk_2, w_uv_2, mla_w_dq_2,
        cq_norm_2, mla_w_uq_2, mla_w_o_2, final_norm_2,
    )


_drawn_inputs = setup_inputs


def setup_inputs(seed=0):
    import zlib

    import numpy as np

    out = dict(_drawn_inputs(seed))
    spreads = {}
    factors = {'gdn_norm_g': 6.115,
     'idx_k_norm_g': 5.148,
     'branch_gate_b': 8.0,
     'norm2_g': 3.099,
     'ffn_conv_b': 2.92,
     'attn_norm_2': 4.992,
     'ffn_norm_2': 2.843,
     'kv_norm_2': 8.0,
     'ckv_norm_2': 8.0,
     'cq_norm_2': 8.0,
     'final_norm_2': 2.79}
    for name, (base, spread) in spreads.items():
        noise = np.random.default_rng([zlib.crc32(name.encode()), seed]).standard_normal(out[name].shape)
        drawn = base * np.exp(spread * noise) if base else spread * noise
        out[name] = __import__('jax').numpy.asarray(drawn.astype(out[name].dtype))
    for name, factor in factors.items():
        out[name] = (out[name] * factor).astype(out[name].dtype)
    return out
```

```python
from contextlib import ExitStack

import numpy as np

import concourse.bass as bass
from concourse import mybir

F32 = mybir.dt.float32
F32R = mybir.dt.float32r
BF16 = mybir.dt.bfloat16
I32 = mybir.dt.int32
ACT = mybir.ActivationFunctionType
ALU = mybir.AluOpType
AX = mybir.AxisListType.X

P = 128
T = 512
NB = T // P
D = 1024
DT = D // P
FF = 2816
FT = FF // P
PAIRS = [(0, 8), (8, 8), (16, 6)]
GH = 8
LEVELS = 7
TOPK = 128
IDXH = 8
EPS = 1e-6
NEG = -1.0e30
FILL = -3.0e38
TAKEN = -3.4e38
PI_F = float(np.float32(3.1415925))
TWO_PI_HI = 6.28125
TWO_PI_LO = 2.0 * np.pi - 6.28125

SEGS = [("gq", 8, 8), ("gk", 8, 8), ("misc", 1, 8), ("gv", 8, 8), ("zga", 16, 8),
        ("idx", 5, 8), ("dkv", 4, 8), ("dqs", 8, 8), ("gb", 8, 8), ("wout", 8, 8),
        ("c0up", 16, 8), ("c0dn", 8, 8), ("c1up", 16, 8), ("c1dn", 8, 8), ("c2up", 12, 8), ("c2dn", 8, 6),
        ("fv", 8, 8), ("ff", 1, 8), ("fqk", 16, 8), ("fo", 8, 8),
        ("s0up", 16, 8), ("s0dn", 8, 8), ("s1up", 16, 8), ("s1dn", 8, 8), ("s2up", 12, 8), ("s2dn", 8, 6),
        ("kva", 3, 8), ("dq", 6, 8), ("uk", 8, 2), ("uv", 8, 2), ("uq", 16, 6), ("mo", 8, 8),
        ("m0up", 16, 8), ("m0dn", 8, 8), ("m1up", 16, 8), ("m1dn", 8, 8), ("m2up", 12, 8), ("m2dn", 8, 6)]
BASE, KT, CNT = {}, {}, {}
_n = 0
for _name, _c, _k in SEGS:
    BASE[_name], CNT[_name], KT[_name] = _n, _c, _k
    _n += _c
PANELS = _n
KT_OF = [k for _, c, k in SEGS for _ in range(c)]

VEC = [("norm1", 8), ("norm2", 8), ("final1", 8), ("an0", 8), ("an0f", 8), ("fn0", 8), ("kvn", 8), ("an1", 8), ("fn1", 8),
       ("final2", 8), ("ckvn", 2), ("cqn", 6), ("gdng", 1), ("gba", 8), ("gbb", 8), ("gconv", 24 * 4),
       ("fconv", 44 * 3), ("fbias", 44), ("ikg", 1), ("alog", 1), ("dtb", 1), ("foxb", 1), ("freq", 1), ("phase", 1)]
VO = {}
_n = 0
for _name, _c in VEC:
    VO[_name] = _n
    _n += _c
NV = _n
MATS = ["ident", "ones", "lastrow", "blk64", "ropesel", "maskT", "maskS"] + [f"lev{l}" for l in range(LEVELS)]
MO = {m: i for i, m in enumerate(MATS)}

NORMS = {"norm1": (8, "x", True), "ikn": (0, "h", True), "norm2": (8, "x", True), "final1": (0, "h", True),
         "an0": (8, "x", True), "fn0": (8, "x", True), "kvn": (8, "x", True), "an1": (8, "y", False),
         "ckvn": (2, "x", True), "cqn": (6, "x", True), "fn1": (8, "x", True), "final2": (8, "h", True)}
LATE = ("norm2", "an0", "fn0", "kvn", "an1", "ckvn", "cqn", "fn1")
ORDER = [("norm1", "norm", 0), ("ikn", "norm", 0), ("gb", "y", 8), ("wout", "sq", 8), ("norm2", "norm", 0),
         ("c", "y", FT), ("c2dn", "sq", 16), ("final1", "norm", 0), ("an0", "norm", 0),
         ("foxo", "ya", 8), ("fo", "sq", 8), ("fn0", "norm", 0), ("s", "y", FT), ("s2dn", "sq", 8),
         ("kvn", "norm", 0), ("an1", "norm", 0), ("ckvsq", "sq", 2), ("ckvn", "norm", 0), ("cqsq", "sq", 6),
         ("cqn", "norm", 0), ("mlao", "ya", 8), ("mo", "sq", 8), ("fn1", "norm", 0), ("m", "y", FT),
         ("m2dn", "sq", 8), ("final2", "norm", 0)]
XR, YR, YH, SQ, NROW, NTMP, NHI = {}, {}, {}, {}, {}, {}, {}
SQ_END = {}
_x = _y = _yh = _sq = _row = _tmp = _hi = 0
for _name, _kind, _c in ORDER:
    XR[_name], YR[_name], YH[_name], SQ[_name] = _x, _y, _yh, _sq
    NROW[_name], NTMP[_name], NHI[_name] = _row, _tmp, _hi
    SQ_END[_name] = _sq
    if _kind == "sq":
        _sq += _c
    if _kind == "y":
        _y += _c
    if _kind in ("y", "ya"):
        _yh += _c
    if _kind == "norm":
        _c, _dst, _own = NORMS[_name]
        _row += _own
        _tmp += _c * (_name not in LATE)
        _hi += _c * (_dst != "h")
        _x += _c * (_dst == "x")
        _y += _c * (_dst == "y")
HIDDEN_BEFORE = {"c": 0, "s": FT, "m": 2 * FT}


def build(nc, I, out, dump=None):
    with ExitStack() as ctx:
        def sb(name, shape, dt=F32):
            return ctx.enter_context(nc.sbuf_tensor("b_" + name, shape, dt))

        def sem(name):
            return ctx.enter_context(nc.semaphore(name))

        h = sb("h", [P, DT, T])
        xh, xl = sb("xh", [P, DT, T], F32R), sb("xl", [P, DT, T], F32R)
        yh, yl = sb("yh", [P, DT, T], F32R), sb("yl", [P, DT, T], F32R)
        raw = sb("raw", [P, 2, DT * P])
        wh, wl = sb("wh", [P, 2, DT * P], F32R), sb("wl", [P, 2, DT * P], F32R)
        vec = sb("vec", [P, NV])
        mats = sb("mats", [P, len(MATS), P])
        identb, maskTb, maskSb = (sb(n, [P, P], BF16) for n in ("identb", "maskTb", "maskSb"))
        ssq = sb("ssq", [P, T])
        diag = sb("diag", [P, T])
        rrow = sb("rrow", [P, T])
        rowT = sb("rowT", [P, NB])
        mhalf = sb("mhalf", [P, 16])
        coef = sb("coef", [P, 2, 32])
        mx = sb("mx", [P, 4])
        nm = sb("nm", [P, 4])
        rs = sb("rs", [P, 4])
        ri = sb("ri", [P, 4])
        top8 = sb("top8", [P, NB * 8])
        state = sb("state", [P, 2, P])
        ARENA = 21888
        arena = sb("arena", [P, ARENA])
        pb = [ctx.enter_context(nc.psum_tensor(f"bank{i}", [P, T], F32)) for i in range(8)]

        def take(off, *dims):
            n = int(np.prod(dims))
            assert off + n <= ARENA, (off, n)
            a = arena[:, off:off + n]
            if len(dims) == 2:
                a = a.rearrange("p (a b) -> p a b", b=dims[1])
            return a

        def V(name, c=0, rows=slice(0, P)):
            if isinstance(c, int):
                return vec[rows, VO[name] + c:VO[name] + c + 1]
            return vec[rows, bass.ds(c + VO[name], 1)]

        def M(name):
            return mats[:, MO[name], :]

        ident, ones = M("ident"), M("ones")

        def tile_of(buf, t, rows=slice(0, P)):
            if isinstance(t, int):
                return buf[rows, t, :]
            return buf[rows, bass.ds(t, 1), :].rearrange("p a b -> p (a b)")

        def bc(ap, n):
            return ap.unsqueeze(2).broadcast_to([ap.shape[0], ap.shape[1], n])

        def rep(ap, n):
            return ap.unsqueeze(1).broadcast_to([ap.shape[0], n, ap.shape[1]])

        def blk(ap):
            return ap.rearrange("p (c t) -> p c t", t=P)

        def B(b):
            return slice(b * P, b * P + P)

        s_const, s_mats, s_x2, s_pos = sem("constants_loaded"), sem("masks_loaded"), sem("x_again"), sem("pos_loaded")
        s_xt = [sem(f"x_loaded{t}") for t in range(DT)]
        first_sq, first_sum = sem("first_squares"), sem("first_squares_summed")
        s_maskb, s_set = sem("bf16_masks"), sem("memsets")
        w_raw = [sem("panel_loaded0"), sem("panel_loaded1")]
        w_hi, w_lo, mm_done, out_free = sem("panel_hi"), sem("panel_lo"), sem("products_done"), sem("bank_read")
        x_ready, y_ready, sq_done, ssq_done = sem("x_tiles"), sem("y_tiles"), sem("squares"), sem("squares_summed")
        n_ms, n_ev, n_pw, n_dg, n_row = (sem("norm_" + n) for n in ("sums", "mean", "rsqrt", "diag", "row"))
        n_tmp, n_hi = sem("norm_scaled"), sem("norm_hi")
        f_ready, gate_mul = sem("qkv_silu"), sem("gate_multiplied")
        gate_silu, prod_done, yh_done = sem("gate_silu"), sem("products_gated"), sem("y_hi")
        s_dump, s_out = sem("dumped"), sem("stored")

        block = ctx.enter_context(nc.Block())

        def wait(eng, s, v, base=0):
            if isinstance(v, int) and v <= 0:
                return
            eng.wait_ge(s, v + base if base else v)

        def loop(eng, n, body):
            body(0)
            if n > 1:
                with eng.Fori(1, n, 1) as i:
                    body(i)

        def each_panel(eng, seg, step):
            base, cnt = BASE[seg], CNT[seg]
            pairs = (cnt - 4) // 2
            done = min(2, cnt)
            for t in range(done):
                step(base + t, t, t // 2, t % 2)
            if pairs > 1:
                with eng.Fori(1, pairs + 1, 1) as q:
                    for r in range(2):
                        step(q * 2 + (base + r), q * 2 + r, q, r)
                done += 2 * pairs
            for t in range(done, cnt):
                step(base + t, t, t // 2, t % 2)

        def load(sp, seg, after=None):
            kt, base = KT[seg], BASE[seg]

            def step(n, t, q, r):
                wait(sp, w_lo, n - 1)
                src = I[seg][t] if isinstance(t, int) else I[seg][bass.ds(t, 1)].rearrange("a p k -> (a p) k")
                sp.dma_start(raw[:, (base + r) % 2, 0:kt * P], src).then_inc(w_raw[(base + r) % 2], 16)
                if after and isinstance(t, int) and t in after:
                    after[t]()
            each_panel(sp, seg, step)

        def split_hi(act, n, half, par, kt):
            act.wait_ge(w_raw[par], (half + 1) * 16)
            wait(act, mm_done, n - 1)
            act.activation(wh[:, par, 0:kt * P], raw[:, par, 0:kt * P], ACT.Copy).then_inc(w_hi, 1)

        def split_lo(dve, n, half, par, kt):
            dve.wait_ge(w_hi, n + 1)
            dve.tensor_tensor(wl[:, par, 0:kt * P], raw[:, par, 0:kt * P], wh[:, par, 0:kt * P].bitcast(F32),
                              ALU.subtract).then_inc(w_lo, 1)

        def split_and(eng, split, seg, post, post_first=False):
            base = BASE[seg]

            def step(n, t, q, r):
                par = (base + r) % 2
                if post is not None and post_first:
                    post(n, t, q, r, pb[par])
                if not isinstance(n, int):
                    split(eng, n + 2, q + ((base + r) // 2 + 1), par, KT[seg])
                elif n + 2 < PANELS:
                    split(eng, n + 2, (n + 2) // 2, par, KT_OF[n + 2])
                if post is not None and not post_first:
                    post(n, t, q, r, pb[par])
            each_panel(eng, seg, step)

        def products(pe, seg, hi, lo, tile0=0, ready=None, between=None):
            kt, base = KT[seg], BASE[seg]

            def step(n, t, q, r):
                par = (base + r) % 2
                bank = pb[par]
                pe.wait_ge(w_lo, n + 1)
                wait(pe, out_free, n - 1)
                for k in range(kt):
                    if ready is not None and isinstance(t, int) and t == 0:
                        pe.wait_ge(ready[0], ready[1] + k + 1)
                    w, x = B(k), tile0 + k
                    pe.matmul(bank[:, :], wh[:, par, w], hi[:, x, :], start=(k == 0), stop=False)
                    pe.matmul(bank[:, :], wh[:, par, w], lo[:, x, :], start=False, stop=False)
                    last = pe.matmul(bank[:, :], wl[:, par, w], hi[:, x, :], start=False, stop=(k == kt - 1))
                    if k == kt - 1:
                        last.then_inc(mm_done, 1)
                    if between and isinstance(t, int) and (t, k) in between:
                        between[t, k]()
            each_panel(pe, seg, step)

        def first_panels(eng, seg, step):
            for t in range(2):
                step(BASE[seg] + t, t, 0, t)

        def split_first(eng, split, seg, post):
            def step(n, t, q, r):
                split(eng, n + 2, (n + 2) // 2, n % 2, KT_OF[n + 2])
                if post is not None:
                    post(n, t, q, r, pb[n % 2])
            first_panels(eng, seg, step)

        def products_first(pe, seg, hi, lo, tile0=0, ready=None):
            def step(n, t, q, r):
                for k in range(KT[seg]):
                    if ready is not None and t == 0:
                        pe.wait_ge(ready[0], ready[1] + k + 1)
                    slice_k(pe, n, n % 2, k, KT[seg], hi, lo, tile0)
            first_panels(pe, seg, step)

        def slice_k(pe, n, par, k, kt, hi, lo, tile0):
            if k == 0:
                pe.wait_ge(w_lo, n + 1)
                wait(pe, out_free, n - 1)
            w, x, bank = B(k), tile0 + k, pb[par]
            pe.matmul(bank[:, :], wh[:, par, w], hi[:, x, :], start=(k == 0), stop=False)
            pe.matmul(bank[:, :], wh[:, par, w], lo[:, x, :], start=False, stop=False)
            last = pe.matmul(bank[:, :], wl[:, par, w], hi[:, x, :], start=False, stop=(k == kt - 1))
            if k == kt - 1:
                last.then_inc(mm_done, 1)

        SCR = 18432
        sqb = take(SCR, 2, T)
        tmpb = take(SCR + 2 * T, 2, T)

        def square(act, name, t, r, src):
            if not isinstance(t, int) or SQ[name] + t > 1:
                act.wait_ge(ssq_done, t + (SQ[name] - 1))
            act.activation(sqb[:, r, :], src, ACT.Square).then_inc(sq_done, 1)

        def sum_squares(pool, name, cnt):
            for t in range(cnt):
                m = SQ[name] + t
                pool.wait_ge(sq_done, m + 1)
                if t == 0:
                    wait(pool, n_ms, NROW[name])
                    pool.tensor_copy(ssq[:, :], sqb[:, 0, :]).then_inc(ssq_done, 1)
                else:
                    pool.wait_ge(ssq_done, m)
                    pool.tensor_tensor(ssq[:, :], ssq[:, :], sqb[:, t % 2, :], ALU.add).then_inc(ssq_done, 1)

        def norm_pe(pe, name, src=None, weights=None, row=True):
            if src is None:
                pe.wait_ge(ssq_done, SQ_END[name])
            for b in range(NB):
                m = pe.matmul(pb[7][:, b:b + 1], (ssq if src is None else src)[:, B(b)],
                              ones[:, 0:1] if weights is None else weights, start=True, stop=True)
            m.then_inc(n_ms, 1)
            if row:
                norm_pe_row(pe, name)

        def norm_pe_row(pe, name):
            pe.wait_ge(n_dg, NROW[name] + 1)
            pe.matmul(pb[6][:, :], ones, diag[:, :], start=True, stop=True).then_inc(n_row, 1)

        def norm_pool(pool, name):
            cnt, dst, own = NORMS[name]
            if own:
                pool.wait_ge(n_ev, NROW[name] + 1)
                pool.tensor_tensor(rowT[:, :], rowT[:, :], mhalf[:, 0:NB], ALU.pow).then_inc(n_pw, 1)
            if dst != "h":
                hi, lo, rdy = (xh, xl, x_ready) if dst == "x" else (yh, yl, y_ready)
                t0 = 2 if name == "cqn" else 0
                for t in range(cnt):
                    pool.wait_ge(n_hi, NHI[name] + t + 1)
                    pool.tensor_tensor(lo[:, t0 + t, :], tmpb[:, t % 2, :], hi[:, t0 + t, :].bitcast(F32),
                                       ALU.subtract).then_inc(rdy, 1)

        def norm_dve(dve, name, src, dim, gain, between=None):
            cnt, dst, own = NORMS[name]
            if own:
                n = NROW[name] + 1
                dve.wait_ge(n_ms, n)
                dve.tensor_scalar(rowT[:, :], pb[7][:, 0:NB], 1.0 / dim, EPS, ALU.mult, ALU.add).then_inc(n_ev, 1)
                dve.wait_ge(n_pw, n)
                dve.tensor_tensor(blk(diag[:, :]), rep(ident, NB), bc(rowT[:, :], P), ALU.mult).then_inc(n_dg, 1)
                if between is not None:
                    between()
                dve.wait_ge(n_row, n)
                dve.tensor_copy(rrow[:, :], pb[6][:, :])
                dve.drain()
            for t in range(cnt):
                if dst == "x" and t >= 2:
                    dve.wait_ge(x_ready, XR[name] + t - 1)
                if dst == "y" and t >= 2:
                    dve.wait_ge(y_ready, YR[name] + t - 1)
                o = h[:, t, :] if dst == "h" else tmpb[:, t % 2, :]
                dve.scalar_tensor_tensor(out=o, in0=src[:, t, :], scalar=V(gain, t), in1=rrow[:, :],
                                         op0=ALU.mult, op1=ALU.mult).then_inc(n_tmp, 1)

        def norm_act(act, name):
            cnt, dst, own = NORMS[name]
            hi = xh if dst == "x" else yh
            t0 = 2 if name == "cqn" else 0
            for t in range(cnt):
                act.wait_ge(n_tmp, NTMP[name] + t + 1)
                act.activation(hi[:, t0 + t, :], tmpb[:, t % 2, :], ACT.Copy).then_inc(n_hi, 1)

        def late_place(name):
            hi, lo, rdy, base = (xh, xl, x_ready, XR) if NORMS[name][1] == "x" else (yh, yl, y_ready, YR)
            return hi, lo, rdy, base[name], 2 if name == "cqn" else 0

        def late_hi(act, name, t, src, gain=None):
            hi, _, _, _, t0 = late_place(name)
            act.activation(tile_of(hi, t + t0 if t0 else t), src, ACT.Copy, scale=V(gain or name, t)).then_inc(n_hi, 1)

        def late_lo(dve, name, t, src, gain=None):
            hi, lo, rdy, base, t0 = late_place(name)
            dve.wait_ge(n_hi, t + (NHI[name] + 1))
            if isinstance(t, int) and t == 0:
                wait(dve, rdy, base)
            tt = t + t0 if t0 else t
            dve.scalar_tensor_tensor(out=tile_of(lo, tt), in0=src, scalar=V(gain or name, t),
                                     in1=tile_of(hi, tt).bitcast(F32), op0=ALU.mult, op1=ALU.subtract).then_inc(rdy, 1)

        def late_pe(pe, name):
            return {(0, 4): lambda: norm_pe(pe, name, row=False), (0, 7): lambda: norm_pe_row(pe, name)}

        def late_pool(pool, name):
            pool.wait_ge(n_ev, NROW[name] + 1)
            pool.tensor_tensor(rowT[:, :], rowT[:, :], mhalf[:, 0:NB], ALU.pow).then_inc(n_pw, 1)

        def late_diag(dve, name, dim):
            n = NROW[name] + 1
            dve.wait_ge(n_ms, n)
            dve.tensor_scalar(rowT[:, :], pb[7][:, 0:NB], 1.0 / dim, EPS, ALU.mult, ALU.add).then_inc(n_ev, 1)
            dve.wait_ge(n_pw, n)
            dve.tensor_tensor(blk(diag[:, :]), rep(ident, NB), bc(rowT[:, :], P), ALU.mult).then_inc(n_dg, 1)

        def late_row(dve, name, dst):
            dve.wait_ge(n_row, NROW[name] + 1)
            dve.tensor_copy(dst, pb[6][:, :])
            dve.drain()

        def add_to_h(dve, name=None, gain=None):
            def post(n, t, q, r, bank):
                dve.wait_ge(mm_done, n + 1)
                if isinstance(t, int) and t == 0:
                    dve.wait_ge(out_free, n)
                dve.tensor_tensor(tile_of(h, t), tile_of(h, t), bank[:, :], ALU.add).then_inc(out_free, 1)
                if name and not (isinstance(t, int) and t == 0):
                    late_lo(dve, name, t - 1, tile_of(h, t - 1), gain)
                    if isinstance(t, int) and t == DT - 1:
                        dve.drain()
                        late_lo(dve, name, t, tile_of(h, t), gain)
            return post

        def square_h(act, sq, name=None, gain=None, scaled=None):
            def post(n, t, q, r, bank):
                if scaled:
                    act.wait_ge(ssq_done, t * 2 + SQ[sq])
                act.wait_ge(out_free, n + 1)
                if name and (isinstance(t, int) or scaled):
                    late_hi(act, name, t, tile_of(h, t), gain)
                if scaled is None:
                    square(act, sq, t, r, tile_of(h, t))
                else:
                    act.activation(sqb[:, 0, :], tile_of(h, t), ACT.Square).then_inc(sq_done, 1)
                    act.activation(sqb[:, 1, :], tile_of(h, t), ACT.Square, scale=V(scaled, t)).then_inc(sq_done, 1)
                if name and not (isinstance(t, int) or scaled):
                    late_hi(act, name, t, tile_of(h, t), gain)
            return post

        def scale_out(dve, dst, off=0):
            def post(n, t, q, r, bank):
                dve.wait_ge(mm_done, n + 1)
                if isinstance(t, int) and t == 0:
                    dve.wait_ge(out_free, n)
                dve.tensor_tensor(tile_of(dst, t + off if off else t), bank[:, :], rrow[:, :], ALU.mult)\
                    .then_inc(out_free, 1)
            return post

        def copy_out(eng, dst, off=0):
            def post(n, t, q, r, bank):
                if isinstance(t, int) and t == 0:
                    eng.wait_ge(out_free, n)
                eng.wait_ge(mm_done, n + 1)
                eng.activation(tile_of(dst, t + off if off else t), bank[:, :], ACT.Copy).then_inc(out_free, 1)
            return post

        sg, cg, cv, pr = (take(j * T, T) for j in range(4))
        raws = [take((4 + j) * T, T) for j in range(2)]
        ssq2 = take(3072, T)
        row2 = take(3584, 2 * NB)
        gate_conv, s_gain = sem("gate_convolved"), sem("gains_multiplied")

        def conv_taps(dve, bank, dst, width, tap, bias):
            if bias is None:
                ins = dve.tensor_scalar(dst, bank, tap(width - 1), None, ALU.mult)
            else:
                ins = dve.tensor_scalar(dst, bank, tap(width - 1), bias, ALU.mult, ALU.add)
            for j in range(width - 2, -1, -1):
                d = width - 1 - j
                dve.drain()
                ins = dve.scalar_tensor_tensor(out=dst[:, d:T], in0=bank[:, 0:T - d], scalar=tap(j),
                                               in1=dst[:, d:T], op0=ALU.mult, op1=ALU.add)
            return ins

        def hidden_dve(dve, l, ch, norm=None):
            first, _ = PAIRS[ch]
            side = {0: 0, 1: FT}

            def post(n, t, q, r, bank):
                p = q + (HIDDEN_BEFORE[l] + first)
                if norm and isinstance(t, int) and t == 0:
                    late_row(dve, norm, rrow[:, :])
                    dve.wait_ge(out_free, n)
                dve.wait_ge(mm_done, n + 1)
                if r == 0:
                    wait(dve, gate_silu, p)
                dst = (cg, cv)[r]
                scaled = raws[r] if l == "c" else dst
                dve.tensor_tensor(scaled, bank[:, :], rrow[:, :], ALU.mult).then_inc(out_free, 1)
                if l == "c":
                    c = q + (first + side[r])
                    dve.drain()
                    last = conv_taps(dve, scaled, dst, 3, lambda j: V("fconv", c * 3 + j), V("fbias", c))
                    if r == 0:
                        last.then_inc(gate_conv, 1)
                if r == 1:
                    dve.drain()
                    dve.wait_ge(gate_silu, p + 1)
                    wait(dve, y_ready, q + (YR[l] + first) if not isinstance(q, int) else q + YR[l] + first)
                    dve.tensor_tensor(pr, sg, cv, ALU.mult).then_inc(prod_done, 1)
            split_and(dve, split_lo, f"{l}{ch}up", post, True)

        def hidden_act(act, l, ch):
            first, cnt = PAIRS[ch]

            def product_hi(q):
                act.wait_ge(prod_done, q + (HIDDEN_BEFORE[l] + first + 1))
                act.activation(tile_of(yh, q), pr, ACT.Copy).then_inc(yh_done, 1)

            def post(n, t, q, r, bank):
                p = q + (HIDDEN_BEFORE[l] + first)
                if r == 0:
                    if not (isinstance(q, int) and q == 0):
                        product_hi(q - 1)
                else:
                    if l == "c":
                        act.wait_ge(gate_conv, q + (first + 1))
                    else:
                        act.wait_ge(out_free, n)
                    wait(act, prod_done, p)
                    act.activation(sg, cg, ACT.Silu).then_inc(gate_silu, 1)
            split_and(act, split_hi, f"{l}{ch}up", post)
            product_hi(cnt - 1)

        def hidden_pool(pool, l, ch):
            first, cnt = PAIRS[ch]

            def body(q):
                pool.wait_ge(yh_done, q + (YH[l] + first + 1))
                pool.tensor_tensor(tile_of(yl, q), pr, tile_of(yh, q).bitcast(F32), ALU.subtract).then_inc(y_ready, 1)
            loop(pool, cnt, body)

        kF, vF = take(0, 8, T), take(4096, 8, T)
        gslot = [[take(8192 + (13 * s + j) * T, T) for j in range(13)] for s in range(2)]
        mT = take(21504, 4, 96)
        eG, egl, dl = (sb(n, [P, NB, GH]) for n in ("eG", "egl", "dl"))
        misc = gslot[1][0]
        (g_mis, g_row1, g_rows, g_mt, g_mts, g_gl, g_e1, g_d, g_e2, g_stage, g_tin, g_diag, g_grow, g_sq, g_ssq,
         g_coef, g_tm, g_kd, g_gsub, g_gam, g_tb, g_fm, g_ka, g_bat, g_t0, g_t0s, g_bm, g_y, g_ys, g_z, g_tu,
         g_uw, g_uws, g_vp, g_vn, g_sp, g_S, g_o, g_osq, g_oss, g_ocf, g_on, g_ot, g_of) = (
            sem("gdn_" + n) for n in
            "misc row1 rows miscT miscTs last exps dif exps2 staged in_tokens diag grow sq ssq coef scaled kd gsub "
            "gamma back features kk_qk gated T0 T0s Bm Y Ys Z TU uw uws vn_sum vn S_sum S o osq oss ocoef on oT oF"
            .split())

        def gconv_dve(dve, seg, dst, col, between=None):
            def post(n, t, q, r, bank):
                if between and isinstance(t, int) and t in between:
                    between[t](dve)
                dve.wait_ge(mm_done, n + 1)
                c = t + col
                if isinstance(t, int):
                    conv_taps(dve, bank[:, :], dst[:, t, :], 4, lambda j: V("gconv", c * 4 + j), None).then_inc(out_free, 1)
                else:
                    d3 = tile_of(dst, t)
                    conv_taps(dve, bank[:, :], d3, 4, lambda j: V("gconv", c * 4 + j), None).then_inc(out_free, 1)
            split_and(dve, split_lo, seg, post, True)

        def gconv_act(act, seg, dst):
            def silu(n, t):
                act.wait_ge(out_free, n + 1)
                act.activation(tile_of(dst, t), tile_of(dst, t), ACT.Silu).then_inc(f_ready, 1)

            def post(n, t, q, r, bank):
                if not (isinstance(t, int) and t == 0):
                    silu(n - 1, t - 1)
            split_and(act, split_hi, seg, post)
            silu(BASE[seg] + 7, 7)

        ra, rb_, rc = gslot[1][1], gslot[1][2], gslot[1][3]
        R8, RB, RW = slice(0, 8), slice(32, 40), slice(64, 72)

        def gmisc_act(act):
            act.activation(misc[RB, :], misc[RB, :], ACT.Sigmoid).then_inc(g_mis, 1)
            act.wait_ge(g_row1, 1)
            act.activation(rb_[R8, :], ra[R8, :], ACT.Abs)
            act.drain()
            act.activation(rb_[R8, :], rb_[R8, :], ACT.Exp, scale=-1.0).then_inc(g_mis, 1)
            act.activation(rowT[R8, 0:1], V("alog", 0, R8), ACT.Exp).then_inc(g_mis, 1)
            act.wait_ge(g_row1, 2)
            act.activation(rb_[R8, :], rb_[R8, :], ACT.Ln).then_inc(g_mis, 1)

        def gexps_act(act):
            act.wait_ge(g_mts, 1)
            act.activation(eG[:, :, :], mT[:, :, 0:GH], ACT.Exp).then_inc(g_e1, 1)
            act.wait_ge(g_d, 1)
            act.activation(dl[:, :, :].rearrange("p a b -> p (a b)"), pb[3][:, 0:NB * GH], ACT.Exp).then_inc(g_e1, 1)
            act.activation(egl[:, :, :], egl[:, :, :], ACT.Exp).then_inc(g_e2, 1)

        def gmisc_dve(dve):
            dve.wait_ge(out_free, BASE["misc"] + 1)
            dve.tensor_scalar(ra[R8, :], misc[R8, :], V("dtb", 0, R8), None, ALU.add).then_inc(g_row1, 1)
            dve.tensor_scalar(misc[RW, :], misc[RW, :], (IDXH ** -0.5) * (64 ** -0.5), None, ALU.mult)
            dve.memset(rc[R8, :], 1.0)
            dve.wait_ge(g_mis, 3)
            dve.tensor_scalar(rb_[R8, :], rb_[R8, :], 1.0, None, ALU.add).then_inc(g_row1, 1)
            dve.tensor_scalar(ra[R8, :], ra[R8, :], 0.0, None, ALU.max)
            dve.tensor_scalar(rowT[R8, 0:1], rowT[R8, 0:1], -1.0, None, ALU.mult)
            dve.wait_ge(g_mis, 4)
            dve.drain()
            dve.tensor_tensor(ra[R8, :], ra[R8, :], rb_[R8, :], ALU.add)
            dve.drain()
            dve.tensor_scalar(ra[R8, :], ra[R8, :], rowT[R8, 0:1], None, ALU.mult)
            dve.drain()
            for b in range(NB):
                ins = dve.tensor_tensor_scan(misc[R8, B(b)], rc[R8, B(b)], ra[R8, B(b)], 0.0, ALU.mult, ALU.add)
            ins.then_inc(g_rows, 1)

        def gcols_dve(dve):
            dve.wait_ge(g_mt, 1)
            dve.tensor_copy(mT, blk(pb[2][:, :])[:, :, 0:96]).then_inc(g_mts, 1)

        def glast_dve(dve):
            dve.wait_ge(g_gl, 1)
            dve.wait_ge(g_mts, 1)
            dve.tensor_tensor(egl[:, :, :], pb[3][:, 0:NB * GH].rearrange("p (a b) -> p a b", b=GH), mT[:, :, 0:GH],
                              ALU.subtract).then_inc(g_d, 1)

        def gmisc_pe(pe):
            pe.wait_ge(g_rows, 1)
            pe.wait_ge(g_mis, 1)
            for b in range(NB):
                m = pe.transpose(pb[2][:, B(b)], misc[:, B(b)], ident)
            m.then_inc(g_mt, 1)

        def glast_pe(pe):
            pe.wait_ge(g_mts, 1)
            pe.matmul(pb[3][:, 0:NB * GH], M("lastrow"), mT[:, :, 0:GH], start=True, stop=True).then_inc(g_gl, 1)

        def hcol(buf, head):
            if isinstance(head, int):
                return buf[:, :, head]
            return buf[:, :, bass.ds(head, 1)].rearrange("p a b -> p (a b)")

        def mcol(off, head):
            if isinstance(head, int):
                return mT[:, :, off + head]
            return mT[:, :, bass.ds(head + off, 1)].rearrange("p a b -> p (a b)")

        QS = 128.0 ** -0.5
        GITER = GH // 2
        LV = range(1, LEVELS)

        def gbanks(s):
            return pb[2 + 3 * s:5 + 3 * s]

        def half_of(ap, l, odd):
            return ap.rearrange("p (m two b) -> p m two b", two=2, b=1 << l)[:, :, odd, :]

        def packed(ap, l):
            return ap.rearrange("p (m b) -> p m b", b=1 << l)

        def gate_panel(i, j):
            n = i * 4 + (BASE["zga"] + j)
            return n, i * 2 + j // 2, i * 2 + (BASE["zga"] + j) // 2, (BASE["zga"] + j) % 2

        def gate_slices(pe, i, j, ks):
            n, t, half, par = gate_panel(i, j)
            for k in ks:
                slice_k(pe, n, par, k, 8, xh, xl, 0)

        def gate_act(act, i, j):
            n, t, half, par = gate_panel(i, j)
            act.wait_ge(mm_done, n + 1)
            act.wait_ge(g_stage, i * 6 + 6)
            dst, func = gate_of[j % 2]
            act.activation(tile_of(dst, t), pb[par][:, :], func, bias=V("gba", t) if j % 2 else 0.0).then_inc(out_free, 1)
            split_hi(act, n + 2, half + 1, par, 8)

        def gate_lo(dve, i, j):
            n, t, half, par = gate_panel(i, j)
            split_lo(dve, n + 2, half + 1, par, 8)

        def gate_dve(dve, first, ready):
            dve.wait_ge(out_free, first * 2 + (BASE["zga"] + 4))
            dve.wait_ge(g_of, ready)
            for r in range(2):
                t = first + r
                dve.tensor_tensor(tile_of(kF, t), tile_of(kF, t), tile_of(vF, t), ALU.mult)
            dve.drain()
            for r in range(2):
                t = first + r
                dve.tensor_tensor(tile_of(h, t), tile_of(h, t), tile_of(kF, t), ALU.mult)

        def gdn_pool(pool):
            pool.wait_ge(g_mts, 1)

            def body(i):
                for s in range(2):
                    S, hd = gslot[s], i * 2 + s
                    if isinstance(i, int):
                        pool.wait_ge(f_ready, 17 + hd)
                    else:
                        pool.wait_ge(f_ready, 24)
                    wait(pool, g_ot, hd - 1)
                    for j, F in enumerate((h, kF, vF)):
                        pool.tensor_copy(S[j], tile_of(F, hd)).then_inc(g_stage, 1)
                pool.wait_ge(g_e2, 1)
                for s in range(2):
                    hd, c = i * 2 + s, coef[:, s, :]
                    pool.wait_ge(g_ssq, hd + 1)
                    pool.tensor_tensor(c[:, 0:8], c[:, 0:8], mhalf[:, 0:8], ALU.pow)
                    pool.drain()
                    pool.tensor_scalar(c[:, 0:4], c[:, 0:4], QS, None, ALU.mult)
                    pool.tensor_tensor(c[:, 8:12], c[:, 4:8], mcol(32, hd), ALU.mult)
                    pool.drain()
                    pool.tensor_tensor(c[:, 12:16], c[:, 0:4], hcol(eG, hd), ALU.mult).then_inc(g_coef, 1)
                for s in range(2):
                    S, hd = gslot[s], i * 2 + s
                    pool.wait_ge(g_tm, hd * 5 + 5)
                    pool.tensor_tensor(blk(S[8]), blk(S[3]), bc(hcol(egl, hd), P), ALU.mult).then_inc(g_kd, 1)
                    pool.tensor_tensor(blk(S[9]), blk(S[4]), bc(hcol(eG, hd), P), ALU.mult).then_inc(g_kd, 1)
                for l in LV:
                    for s in range(2):
                        S, hd = gslot[s], i * 2 + s
                        if l == 1:
                            pool.wait_ge(g_bat, hd * 3 + 3)
                        if l >= 3:
                            pool.wait_ge(g_y, i * 12 + (2 * (l - 3) + s + 1))
                        pool.tensor_tensor(blk(S[2] if l % 2 else S[11]), blk(S[4]), rep(M(f"lev{l}"), NB), ALU.mult)\
                            .then_inc(g_bm, 1)
                for s in range(2):
                    hd = i * 2 + s
                    pool.wait_ge(g_oss, hd + 1)
                    pool.tensor_tensor(coef[:, s, 16:20], coef[:, s, 16:20], mhalf[:, 0:4], ALU.pow).then_inc(g_ocf, 1)
            loop(pool, GITER, body)

        def gdn_pe(pe):
            pe.wait_ge(s_maskb, 3)
            pe.wait_ge(g_e2, 1)

            def mm4(bank, lhs, rhs):
                for c in range(NB):
                    m = pe.matmul(bank[:, B(c)], lhs[:, B(c)], rhs[:, B(c)], start=True, stop=True)
                return m

            def mm4_half(bank, lhs, rhs, l, odd):
                for c in range(NB):
                    m = pe.matmul(packed(bank[:, c * 64:c * 64 + 64], l), lhs[:, B(c)], half_of(rhs[:, B(c)], l, odd),
                                  start=True, stop=True)
                return m

            def tr4(bank, src):
                for c in range(NB):
                    m = pe.transpose(bank[:, B(c)], src[:, B(c)], ident)
                return m

            def body(i):
                gate_slices(pe, i, 0, range(0, 4))
                for s in range(2):
                    S, hd, b = gslot[s], i * 2 + s, gbanks(s)
                    wait(pe, g_of, hd - 1)
                    pe.wait_ge(g_diag, hd + 1)
                    pe.matmul(b[2][:, :], identb[:, :], rep(maskTb[:, :], NB), start=True, stop=False)
                    pe.matmul(b[2][:, :], ones, S[11], start=False, stop=True).then_inc(g_grow, 1)
                    for j in range(2):
                        pe.wait_ge(g_stage, hd * 3 + (j + 1))
                        tr4(b[j], S[j]).then_inc(g_tin, 1)
                for s in range(2):
                    S, hd, b = gslot[s], i * 2 + s, gbanks(s)
                    pe.wait_ge(g_stage, hd * 3 + 3)
                    pe.wait_ge(g_gsub, hd + 1)
                    tr4(b[2], S[2]).then_inc(g_tin, 1)
                gate_slices(pe, i, 0, range(4, 8))
                for s in range(2):
                    S, hd, b = gslot[s], i * 2 + s, gbanks(s)
                    pe.wait_ge(g_tm, hd * 5 + 5)
                    for j, src in enumerate((3, 4, 5)):
                        tr4(b[j], S[src]).then_inc(g_tb, 1)
                for s in range(2):
                    S, hd, b = gslot[s], i * 2 + s, gbanks(s)
                    pe.wait_ge(g_fm, i * 8 + (3 * s + 1))
                    tr4(b[0], S[6]).then_inc(g_tb, 1)
                for s in range(2):
                    S, hd, b = gslot[s], i * 2 + s, gbanks(s)
                    pe.wait_ge(g_fm, i * 8 + (3 * s + 3))
                    mm4(b[1], S[0], S[1]).then_inc(g_ka, 1)
                    mm4(b[2], S[0], S[2]).then_inc(g_ka, 1)
                gate_slices(pe, i, 1, range(0, 4))
                for s in range(2):
                    S, hd, b = gslot[s], i * 2 + s, gbanks(s)
                    pe.wait_ge(g_fm, i * 8 + (7 + s))
                    pe.wait_ge(g_bat, hd * 3 + 3)
                    tr4(b[0], S[12]).then_inc(g_t0, 1)
                gate_slices(pe, i, 1, range(4, 6))
                for l in LV:
                    for s in range(2):
                        S, hd, b = gslot[s], i * 2 + s, gbanks(s)
                        pe.wait_ge(g_bm, i * 12 + (2 * (l - 1) + s + 1))
                        if l == 1:
                            pe.wait_ge(g_t0s, hd + 1)
                        else:
                            pe.wait_ge(g_tu, i * 22 + (4 * (l - 2) + 2 * (s + 1)))
                        mm4(b[2], S[2] if l % 2 else S[11], S[6]).then_inc(g_y, 1)
                    if l < LEVELS - 1:
                        gate_slices(pe, i, 1 if l == 1 else 2, [6] if l == 1 else [2 * (l - 2)])
                    for s in range(2):
                        S, hd, b = gslot[s], i * 2 + s, gbanks(s)
                        pe.wait_ge(g_ys, i * 12 + (2 * (l - 1) + s + 1))
                        if l < LEVELS - 1:
                            mm4_half(b[0], S[12], S[10], l, 0)
                        mm4_half(b[1], S[10], S[12], l, 1).then_inc(g_z, 1)
                    if l < LEVELS - 1:
                        gate_slices(pe, i, 1 if l == 1 else 2, [7] if l == 1 else [2 * (l - 2) + 1])
                for s in range(2):
                    S, hd, b = gslot[s], i * 2 + s, gbanks(s)
                    pe.wait_ge(g_tu, i * 22 + (4 * (LEVELS - 2) + s + 1))
                    mm4(b[2], S[12], S[7]).then_inc(g_uw, 1)
                    mm4(b[0], S[9], S[12]).then_inc(g_uw, 1)
                for c in range(NB):
                    for s in range(2):
                        S, hd, b = gslot[s], i * 2 + s, gbanks(s)
                        if c == 0:
                            pe.wait_ge(g_uws, hd * 2 + 2)
                        if c > 0:
                            pe.wait_ge(g_S, i * 6 + (2 * (c - 1) + s + 1))
                            pe.matmul(b[0][:, 0:P], S[1][:, B(c)], state[:, s, :], start=True, stop=True)\
                                .then_inc(g_vp, 1)
                            pe.matmul(b[2][:, B(c)], S[3][:, B(c)], state[:, s, :], start=True, stop=False)
                    gate_slices(pe, i, 3, [2 * c])
                    for s in range(2):
                        S, hd, b = gslot[s], i * 2 + s, gbanks(s)
                        if c > 0:
                            pe.wait_ge(g_vn, i * 6 + (2 * (c - 1) + s + 1))
                        m = pe.matmul(b[2][:, B(c)], S[5][:, B(c)], S[0][:, B(c)], start=(c == 0), stop=True)
                        if c == NB - 1:
                            m.then_inc(g_o, 1)
                        else:
                            pe.matmul(b[1][:, 0:P], S[8][:, B(c)], S[0][:, B(c)], start=True, stop=True)\
                                .then_inc(g_sp, 1)
                    gate_slices(pe, i, 3, [2 * c + 1])
                for s in range(2):
                    S, hd, b = gslot[s], i * 2 + s, gbanks(s)
                    pe.wait_ge(g_on, hd + 1)
                    tr4(b[0], S[11]).then_inc(g_ot, 1)
            loop(pe, GITER, body)

        def gdn_act(act):
            def body(i):
                for s in range(2):
                    S, hd, b = gslot[s], i * 2 + s, gbanks(s)
                    act.wait_ge(g_tin, i * 6 + (2 * s + 2))
                    act.activation(S[10], b[0][:, :], ACT.Square).then_inc(g_sq, 1)
                    act.activation(S[12], b[1][:, :], ACT.Square).then_inc(g_sq, 1)
                for s in range(2):
                    act.wait_ge(g_gsub, i * 2 + (s + 1))
                    act.activation(gslot[s][11], gslot[s][11], ACT.Exp).then_inc(g_gam, 1)
                for s in range(2):
                    S, hd, b = gslot[s], i * 2 + s, gbanks(s)
                    for j in range(3):
                        act.wait_ge(g_tb, i * 8 + (3 * s + j + 1))
                        act.activation(S[j], b[j][:, :], ACT.Copy).then_inc(g_fm, 1)
                for s in range(2):
                    S, hd, b = gslot[s], i * 2 + s, gbanks(s)
                    act.wait_ge(g_tb, i * 8 + (7 + s))
                    act.wait_ge(g_kd, hd * 2 + 2)
                    act.activation(S[3], b[0][:, :], ACT.Copy).then_inc(g_fm, 1)
                gate_act(act, i, 0)
                for s in range(2):
                    S, hd, b = gslot[s], i * 2 + s, gbanks(s)
                    act.wait_ge(g_t0, hd + 1)
                    act.activation(S[6], b[0][:, :], ACT.Copy).then_inc(g_t0s, 1)
                for l in LV:
                    for s in range(2):
                        S, b = gslot[s], gbanks(s)
                        act.wait_ge(g_y, i * 12 + (2 * (l - 1) + s + 1))
                        act.activation(S[10], b[2][:, :], ACT.Copy).then_inc(g_ys, 1)
                    if l == 2:
                        gate_act(act, i, 1)
                for s in range(2):
                    S, hd, b = gslot[s], i * 2 + s, gbanks(s)
                    act.wait_ge(g_uw, hd * 2 + 1)
                    act.activation(S[0], b[2][:, :], ACT.Copy).then_inc(g_uws, 1)
                    act.wait_ge(g_uw, hd * 2 + 2)
                    act.activation(S[1], b[0][:, :], ACT.Copy, scale=-1.0).then_inc(g_uws, 1)
                gate_act(act, i, 2)
                for s in range(2):
                    S, hd, b = gslot[s], i * 2 + s, gbanks(s)
                    act.wait_ge(g_o, hd + 1)
                    act.activation(S[2], b[2][:, :], ACT.Square).then_inc(g_osq, 1)
                gate_act(act, i, 3)
                for s in range(2):
                    hd, b = i * 2 + s, gbanks(s)
                    act.wait_ge(g_ot, hd + 1)
                    act.activation(tile_of(h, hd), b[0][:, :], ACT.Copy, scale=V("gdng")).then_inc(g_of, 1)
            loop(act, GITER, body)

        def gdn_dve(dve):
            def body(i):
                for s in range(2):
                    S, hd = gslot[s], i * 2 + s
                    wait(dve, g_ot, hd - 1)
                    dve.tensor_tensor(blk(S[11]), rep(ident, NB), bc(mcol(0, hd), P), ALU.mult).then_inc(g_diag, 1)
                for s in range(2):
                    S, hd, b = gslot[s], i * 2 + s, gbanks(s)
                    dve.wait_ge(g_grow, hd + 1)
                    dve.tensor_tensor(blk(S[11]), blk(b[2][:, :]), bc(mcol(0, hd), P), ALU.subtract).then_inc(g_gsub, 1)
                for s in range(2):
                    S, hd, b = gslot[s], i * 2 + s, gbanks(s)
                    dve.wait_ge(g_sq, hd * 2 + 2)
                    dve.tensor_reduce(coef[:, s, 0:4], blk(S[10]), AX, ALU.add)
                    dve.tensor_reduce(coef[:, s, 4:8], blk(S[12]), AX, ALU.add)
                    dve.drain()
                    dve.tensor_scalar(coef[:, s, 0:8], coef[:, s, 0:8], EPS, None, ALU.add).then_inc(g_ssq, 1)
                for s in range(2):
                    S, hd, b, c = gslot[s], i * 2 + s, gbanks(s), coef[:, s, :]
                    dve.wait_ge(g_coef, hd + 1)
                    dve.wait_ge(g_tin, i * 6 + (5 + s))
                    for dst, bank, k in ((3, 1, c[:, 4:8]), (4, 1, c[:, 8:12]), (5, 0, c[:, 0:4]), (6, 0, c[:, 12:16]),
                                         (7, 2, mcol(32, hd))):
                        dve.tensor_tensor(blk(S[dst]), blk(b[bank][:, :]), bc(k, P), ALU.mult).then_inc(g_tm, 1)
                gate_lo(dve, i, 0)
                for s in range(2):
                    S, hd, b = gslot[s], i * 2 + s, gbanks(s)
                    dve.wait_ge(g_gam, hd + 1)
                    dve.wait_ge(g_kd, hd * 2 + 2)
                    dve.wait_ge(g_ka, hd * 2 + 1)
                    dve.tensor_tensor(S[4], b[1][:, :], S[11], ALU.mult).then_inc(g_bat, 1)
                    dve.wait_ge(g_ka, hd * 2 + 2)
                    dve.tensor_tensor(S[5], b[2][:, :], S[11], ALU.mult).then_inc(g_bat, 1)
                    dve.wait_ge(g_bat, hd * 3 + 1)
                    dve.tensor_tensor(blk(S[10]), blk(S[4]), rep(M("lev0"), NB), ALU.mult)
                    dve.drain()
                    dve.tensor_tensor(blk(S[12]), rep(ident, NB), blk(S[10]), ALU.subtract).then_inc(g_bat, 1)
                for l in LV:
                    for s in range(2):
                        S, hd, b = gslot[s], i * 2 + s, gbanks(s)
                        dve.wait_ge(g_z, i * 12 + (2 * (l - 1) + s + 1))
                        if l < LEVELS - 1:
                            even = half_of(S[6], l, 0)
                            dve.tensor_tensor(even, even, packed(b[0][:, 0:256], l), ALU.subtract).then_inc(g_tu, 1)
                        odd = half_of(S[12], l, 1)
                        dve.tensor_tensor(odd, odd, packed(b[1][:, 0:256], l), ALU.subtract).then_inc(g_tu, 1)
                    if l == 2:
                        gate_lo(dve, i, 1)
                    if l == 4 and not (isinstance(i, int) and i == 0):
                        gate_dve(dve, i * 2 - 2, i * 2)
                for c in range(NB):
                    for s in range(2):
                        S, hd, b = gslot[s], i * 2 + s, gbanks(s)
                        if c > 0:
                            dve.wait_ge(g_vp, i * 6 + (2 * (c - 1) + s + 1))
                            if c == 1:
                                dve.wait_ge(g_uws, hd * 2 + 2)
                            dve.tensor_tensor(S[0][:, B(c)], S[0][:, B(c)], b[0][:, 0:P], ALU.add).then_inc(g_vn, 1)
                    for s in range(2):
                        S, hd, b = gslot[s], i * 2 + s, gbanks(s)
                        if c == NB - 1:
                            continue
                        dve.wait_ge(g_sp, i * 6 + (2 * c + s + 1))
                        if c == 0:
                            dve.tensor_copy(state[:, s, :], b[1][:, 0:P]).then_inc(g_S, 1)
                        else:
                            dve.wait_ge(g_S, i * 6 + (2 * (c - 1) + s + 1))
                            d1 = dl[:, c, hd:hd + 1] if isinstance(hd, int) else dl[:, c, bass.ds(hd, 1)]
                            dve.scalar_tensor_tensor(out=state[:, s, :], in0=state[:, s, :], scalar=d1,
                                                     in1=b[1][:, 0:P], op0=ALU.mult, op1=ALU.add).then_inc(g_S, 1)
                    if c == 0:
                        gate_lo(dve, i, 2)
                for s in range(2):
                    S, hd, b = gslot[s], i * 2 + s, gbanks(s)
                    dve.wait_ge(g_osq, hd + 1)
                    dve.tensor_reduce(coef[:, s, 16:20], blk(S[2]), AX, ALU.add)
                    dve.drain()
                    dve.tensor_scalar(coef[:, s, 16:20], coef[:, s, 16:20], 1.0 / P, EPS, ALU.mult, ALU.add)\
                        .then_inc(g_oss, 1)
                for s in range(2):
                    S, hd, b = gslot[s], i * 2 + s, gbanks(s)
                    dve.wait_ge(g_ocf, hd + 1)
                    dve.tensor_tensor(blk(S[11]), blk(b[2][:, :]), bc(coef[:, s, 16:20], P), ALU.mult).then_inc(g_on, 1)
                gate_lo(dve, i, 3)
            loop(dve, GITER, body)

        gate_of = {0: (kF, ACT.Silu), 1: (vF, ACT.Sigmoid)}

        DS = take(0, 17, T)
        vD = take(8704, NB, 256)
        mask = take(9728, NB, T)
        oD = take(11776, 8, T)
        rl, ikn, xc, sqk = take(15872, 2, T), take(16896, T), take(17408, T), take(17920, T)
        i_mean, i_xc, i_sq, i_kn, i_s, i_r, i_acc, i_cs, i_mask = (
            sem("idx_" + n) for n in "mean centred squares k_normed dots relu summed causal mask".split())
        SCORES = [(i, hh) for i in range(1, NB) for hh in range(IDXH)]

        def index_pe(pe):
            pe.wait_ge(out_free, BASE["idx"] + CNT["idx"])
            pe.matmul(pb[2][:, :], M("blk64"), DS[:, 16, :], start=True, stop=True).then_inc(i_mean, 1)
            pe.wait_ge(i_sq, 1)
            norm_pe(pe, "ikn", sqk, M("blk64")[:, 0:1], row=False)
            products(pe, "dkv", xh, xl)
            norm_pe_row(pe, "ikn")
            pe.wait_ge(i_kn, 1)
            for u, (i, hh) in enumerate(SCORES):
                rows = slice(64 * (hh % 2), 64 * (hh % 2) + 64)
                wait(pe, i_r, u - 1)
                pe.matmul(pb[2 + u % 2][:, 0:(i + 1) * P], DS[rows, 12 + hh // 2, B(i)], ikn[rows, 0:(i + 1) * P],
                          start=True, stop=True).then_inc(i_s, 1)

        def index_act(act):
            act.wait_ge(i_xc, 1)
            act.activation(sqk, xc, ACT.Square).then_inc(i_sq, 1)
            split_and(act, split_hi, "dkv", copy_out(act, DS, 8))
            for u, (i, hh) in enumerate(SCORES):
                act.wait_ge(i_s, u + 1)
                wait(act, i_acc, u - 1)
                nk = (i + 1) * P
                act.activation(rl[:, u % 2, 0:nk], pb[2 + u % 2][:, 0:nk], ACT.Relu).then_inc(i_r, 1)

        def index_pool(pool):
            norm_pool(pool, "ikn")
            for i in range(1, NB):
                pool.wait_ge(i_acc, IDXH * i)
                d = mask[:, i, B(i)]
                pool.affine_select(out=d, in_=d, compare_op=ALU.is_ge, fill=FILL, base=0, pattern=[[-1, P]],
                                   channel_multiplier=1).then_inc(i_cs, 1)

        def index_dve(dve):
            dve.wait_ge(i_mean, 1)
            dve.tensor_tensor(xc, DS[:, 16, :], pb[2][:, :], ALU.subtract).then_inc(i_xc, 1)
            norm_dve(dve, "ikn", None, 1, None, lambda: split_and(dve, split_lo, "dkv", None))
            dve.scalar_tensor_tensor(out=ikn, in0=xc, scalar=V("ikg"), in1=rrow[:, :], op0=ALU.mult, op1=ALU.mult)\
                .then_inc(i_kn, 1)
            dve.tensor_copy(mask[:, 0, B(0)], M("maskS"))
            for u, (i, hh) in enumerate(SCORES):
                dve.wait_ge(i_r, u + 1)
                nk, w = (i + 1) * P, mT[:, i, 64 + hh:65 + hh]
                if hh == 0:
                    dve.tensor_scalar(mask[:, i, 0:nk], rl[:, u % 2, 0:nk], w, None, ALU.mult).then_inc(i_acc, 1)
                else:
                    dve.wait_ge(i_acc, u)
                    dve.scalar_tensor_tensor(out=mask[:, i, 0:nk], in0=rl[:, u % 2, 0:nk], scalar=w,
                                             in1=mask[:, i, 0:nk], op0=ALU.mult, op1=ALU.add).then_inc(i_acc, 1)
            dve.wait_ge(i_cs, NB - 1)
            blocks = [(mask[:, i, 0:(i + 1) * P], top8[:, i * 8:i * 8 + 8]) for i in range(1, NB)]

            def take8():
                for sc, t8 in blocks:
                    dve.max(t8, sc)
                dve.drain()
                for sc, t8 in blocks:
                    dve.match_replace(sc, t8, sc, TAKEN)
                dve.drain()
            with dve.Fori(0, TOPK // 16, 1):
                take8()
                take8()
            for sc, _ in blocks:
                dve.tensor_scalar(sc, sc, (FILL + TAKEN) / 2, NEG, ALU.is_gt, ALU.mult).then_inc(i_mask, 1)

        v_t, v_ea, v_ed = sem("v_transposed"), sem("v_copied_act"), sem("v_copied_dve")

        def v_pe(pe, tiles, done):
            for t, src in enumerate(tiles):
                if t >= 4:
                    s_, k = ((v_ea, v_ed)[t % 2], (done + t - 4) // 2 + 1)
                    pe.wait_ge(s_, k)
                for b in range(NB):
                    m = pe.transpose(pb[2 + t % 4][:, B(b)], src[:, B(b)], ident)
                m.then_inc(v_t, 1)

        def v_copy(eng, odd, n, dst, done):
            for t in range(odd, n, 2):
                eng.wait_ge(v_t, done + t + 1)
                a, b = dst[:, :, B(t)], blk(pb[2 + t % 4][:, :])
                if odd:
                    eng.tensor_copy(a, b).then_inc(v_ed, 1)
                else:
                    eng.activation(a, b, ACT.Copy).then_inc(v_ea, 1)

        a_st, a_dg, a_cp, a_cr, a_s, a_l, a_p, a_t, a_te, a_o, a_oe, a_ot, a_of = (
            sem("attn_" + n) for n in "staged decay_diag decay_row decay_copied logits shifted probs transposed "
            "transposed_copied out out_scaled outT outT_copied".split())
        spare = mats[:, MO["lev0"]:MO["lev0"] + 4, :]
        UNITS_BEFORE = {"dsa": 0, "fox": 32, "mla": 96}
        STAGED_BEFORE = {"dsa": 0, "fox": 8, "mla": 24}
        TILES_BEFORE = {"dsa": 0, "fox": 8, "mla": 16}

        class Attention:

            def __init__(self, name, iters, heads, dv, scale, probs, probsT, outs, group, fill):
                self.name, self.iters, self.heads, self.dv, self.scale = name, iters, heads, dv, scale
                self.probs, self.probsT, self.outs, self.group = probs, probsT, outs, group
                self.units = [(s, i) for s in range(heads) for i in range(NB)]
                self.U = len(self.units)
                self.ub, self.sb_, self.tb = UNITS_BEFORE[name], STAGED_BEFORE[name], TILES_BEFORE[name]
                self.G = self.U // group
                self.seg, self.f0, self.per, self.filled, self.operand = fill
                kt = KT[self.seg]
                slices = [(j, k) for j in range(self.per) for k in range(kt)]
                self.pre = {"dsa": 0, "fox": 6, "mla": 4}[name]
                self.at = {-1: slices[0:self.pre]}
                for u in range(self.U):
                    self.at[u] = slices[self.pre + 2 * u:self.pre + 2 * u + 2]
                self.done = {j: max(u for u, x in self.at.items() if (j, kt - 1) in x) for j in range(self.per)}
                self.last_filled = lambda it: isinstance(it, int) and it >= self.filled

            def panel(self, it, j):
                t = it * self.per + (self.f0 + j)
                n = it * self.per + (BASE[self.seg] + self.f0 + j)
                if isinstance(n, int):
                    return n, t, n // 2, n % 2
                half = it * (self.per // 2) + (BASE[self.seg] + self.f0 + j) // 2
                return n, t, half, (BASE[self.seg] + self.f0 + j) % 2

        def heads_loop(eng, A, body):
            body(0)
            if A.iters > 3:
                with eng.Fori(1, A.iters - 2, 1) as it:
                    body(it)
            for it in range(max(1, A.iters - 2), A.iters):
                body(it)

        def fill_pe(pe, A, it, u):
            if A.last_filled(it):
                return []
            hi, lo, tile0 = A.operand

            def run(j, k):
                n, t, half, par = A.panel(it, j)
                slice_k(pe, n, par, k, KT[A.seg], hi, lo, tile0)
            return [lambda j=j, k=k: run(j, k) for j, k in A.at[u]]

        def fill_post(eng, split, A, it, u, post, later=0):
            if A.last_filled(it):
                return
            for j in range(A.per):
                n, t, half, par = A.panel(it, j)
                if A.done[j] == u - 1 and post is not None:
                    post(n, t, it, j, pb[par])
                if min(A.done[j] + later, A.U - 1) == u - 1:
                    split(eng, n + 2, half + 1, par, KT_OF[n + 2] if isinstance(n, int) else KT[A.seg])

        def crow_dve(dve, m):
            wait(dve, a_cp, m)
            col = cT[:, :, m] if isinstance(m, int) else cT[:, :, bass.ds(m, 1)].rearrange("p a b -> p (a b)")
            dve.tensor_tensor(blk(fdiag), rep(ident, NB), bc(col, P), ALU.mult).then_inc(a_dg, 1)

        def crow_pe(pe, m):
            pe.wait_ge(a_dg, m + 1)
            wait(pe, a_cr, m)
            pe.matmul(pb[5][:, :], ones, fdiag, start=True, stop=True).then_inc(a_cp, 1)

        def crow_act(act, m, s):
            act.wait_ge(a_cp, m + 1)
            act.activation(crow[s], pb[5][:, :], ACT.Copy).then_inc(a_cr, 1)

        def attn_pe(pe, A, q_ap, k_ap, v_ap, stages):
            bank_free = a_p if A.name == "mla" else a_l

            def body(it):
                more = not (isinstance(it, int) and it == A.iters - 1)

                def W(s_, v, base):
                    v = it * A.U + v
                    wait(pe, s_, v, base) if not isinstance(v, int) else wait(pe, s_, v, base if v > 0 else 0)

                def dots(u, it=it):
                    def W(s_, v, base):
                        v = it * A.U + v
                        wait(pe, s_, v, base if not isinstance(v, int) or v > 0 else 0)
                    s, i = A.units[u]
                    W(bank_free, u - 1, A.ub)
                    bank, nk = pb[2 + u % 2], (i + 1) * P
                    masked = A.name != "dsa"
                    if masked:
                        m = pe.matmul(bank[:, 0:nk], q_ap(s, i), k_ap(it, s, nk), start=True, stop=False)
                        m = pe.matmul(bank[:, B(i)], identb[:, :], maskSb[:, :], start=False, stop=True)
                    else:
                        m = pe.matmul(bank[:, 0:nk], q_ap(s, i), k_ap(it, s, nk), start=True, stop=True)
                    m.then_inc(a_s, 1)

                def turn(u):
                    s, i = A.units[u]
                    W(a_p, u + 1, A.ub)
                    W(a_te, u, A.ub)
                    for j in range(i + 1):
                        m = pe.transpose(pb[4][:, B(j)], A.probs[u % 2][:, B(j)], ident)
                    m.then_inc(a_t, 1)

                def values(u):
                    s, i = A.units[u]
                    W(a_te, u + 1, A.ub)
                    W(a_oe, u - 1, A.ub)
                    for j in range(i + 1):
                        m = pe.matmul(pb[6 + u % 2][:, 0:A.dv], A.probsT[u % 2][:, B(j)], v_ap(it, s, j),
                                      start=(j == 0), stop=(j == i))
                    m.then_inc(a_o, 1)

                def finish(g):
                    W(a_oe, (g + 1) * A.group, A.ub)
                    n = it * A.G + g
                    wait(pe, a_of, n, A.tb)
                    if A.name == "fox" and more:
                        pe.wait_ge(a_cr, it * 2 + 4)
                    for b in range(NB):
                        m = pe.transpose(pb[5][:, B(b)], A.outs[g % len(A.outs)][:, b, :], ident)
                    m.then_inc(a_ot, 1)

                def first_dots(it):
                    pe.wait_ge(a_st, it * stages + (A.sb_ + stages))
                    dots(0, it)
                    dots(1, it)

                if isinstance(it, int) and it == 0:
                    first_dots(0)
                    for f in fill_pe(pe, A, it, -1):
                        f()
                ahead = fill_pe(pe, A, it + 1, -1) if more else []

                def ahead_next(cnt):
                    for f in ahead[0:cnt]:
                        f()
                    del ahead[0:cnt]
                for u in range(A.U):
                    fills = fill_pe(pe, A, it, u)
                    turn(u)
                    for f in fills[0:1]:
                        f()
                    if u + 1 == A.U:
                        ahead_next(1)
                    if u + 2 < A.U:
                        dots(u + 2)
                    elif u + 1 == A.U and more:
                        first_dots(it + 1)
                    for f in fills[1:]:
                        f()
                    if u >= 1:
                        values(u - 1)
                    if u >= 2 and (u - 1) % A.group == 0:
                        finish((u - 1) // A.group - 1)
                    if A.name == "fox" and more and u in (4, 6):
                        if u == 4:
                            wait(pe, a_of, it, A.tb if not isinstance(it, int) or it else 0)
                        crow_pe(pe, it * 2 + (2 + (u == 6)))
                ahead_next(1)
                values(A.U - 1)
                ahead_next(len(ahead))
                finish(A.G - 1)
            heads_loop(pe, A, body)

        def attn_act(act, A, out_tile, post, pairs, extra=None):
            def body(it):
                more = not (isinstance(it, int) and it == A.iters - 1)

                def W(s_, v, base):
                    v = it * A.U + v
                    wait(act, s_, v, base if not isinstance(v, int) or v > 0 else 0)

                def expo(u, it=it):
                    def W(s_, v, base):
                        v = it * A.U + v
                        wait(act, s_, v, base if not isinstance(v, int) or v > 0 else 0)
                    s, i = A.units[u]
                    W(a_l, u + 1, A.ub)
                    W(a_t, u - 1, A.ub)
                    W(a_oe, u - 3, A.ub)
                    nk, c = (i + 1) * P, slice(u % 4, u % 4 + 1)
                    src = pb[2 + u % 2][:, 0:nk] if A.name == "mla" else lring[u % 2][:, 0:nk]
                    act.activation(A.probs[u % 2][:, 0:nk], src, ACT.Exp, bias=nm[:, c],
                                   scale=A.scale if A.name == "mla" else 1.0, accum_out=rs[:, c]).then_inc(a_p, 1)

                def copyT(u):
                    s, i = A.units[u]
                    W(a_t, u + 1, A.ub)
                    W(a_o, u - 1, A.ub)
                    nk = (i + 1) * P
                    act.activation(A.probsT[u % 2][:, 0:nk], pb[4][:, 0:nk], ACT.Copy).then_inc(a_te, 1)

                def finish(g):
                    n = it * A.G + g
                    act.wait_ge(a_ot, n + (A.tb + 1))
                    if A.name == "dsa":
                        act.activation(out_tile(n), pb[5][:, :], ACT.Copy).then_inc(a_of, 1)
                    else:
                        act.activation(out_tile(n), pb[5][:, :], ACT.Copy).then_inc(yh_done, 1)

                if isinstance(it, int) and it == 0:
                    expo(0)
                for u in range(A.U):
                    if u + 1 < A.U:
                        expo(u + 1)
                    copyT(u)
                    fill_post(act, split_hi, A, it, u, post)
                    if more and u == A.U - 2:
                        stage_act(act, A, it + 1, pairs(it + 1))
                    if A.name == "fox" and more and u == 5:
                        crow_act(act, it * 2 + 2, 0)
                    if u >= 2 and (u - 1) % A.group == 0:
                        finish((u - 1) // A.group - 1)
                fill_post(act, split_hi, A, it, A.U, post)
                if A.name == "fox" and more:
                    crow_act(act, it * 2 + 3, 1)
                if more:
                    expo(0, it + 1)
                finish(A.G - 1)
                if extra and isinstance(it, int) and it == 0:
                    extra()
            stage_act(act, A, 0, pairs(0))
            heads_loop(act, A, body)

        def attn_dve(dve, A, out_cols, post, extra=None):
            def body(it):
                more = not (isinstance(it, int) and it == A.iters - 1)

                def W(s_, v, base):
                    v = it * A.U + v
                    wait(dve, s_, v, base if not isinstance(v, int) or v > 0 else 0)

                def logits(u, it=it):
                    def W(s_, v, base):
                        v = it * A.U + v
                        wait(dve, s_, v, base if not isinstance(v, int) or v > 0 else 0)
                    s, i = A.units[u]
                    W(a_s, u + 1, A.ub)
                    W(a_p, u - 1, A.ub)
                    nk, c, bank = (i + 1) * P, slice(u % 4, u % 4 + 1), pb[2 + u % 2]
                    if A.name == "mla":
                        dve.tensor_reduce(mx[:, c], bank[:, 0:nk], AX, ALU.max)
                    else:
                        L = lring[u % 2][:, 0:nk]
                        in1, op = (mask[:, i, 0:nk], ALU.add) if A.name == "dsa" else (crow[s][:, 0:nk], ALU.subtract)
                        if A.name == "fox":
                            dve.wait_ge(a_cr, it * 2 + (s + 1))
                        dve.scalar_tensor_tensor(out=L, in0=bank[:, 0:nk], scalar=A.scale, in1=in1, op0=ALU.mult, op1=op)
                        dve.drain()
                        dve.tensor_reduce(mx[:, c], L, AX, ALU.max)
                    dve.drain()
                    dve.tensor_scalar(nm[:, c], mx[:, c], -A.scale if A.name == "mla" else -1.0, None, ALU.mult)\
                        .then_inc(a_l, 1)

                def scaled(u):
                    s, i = A.units[u]
                    c = slice(u % 4, u % 4 + 1)
                    g = u // A.group
                    if u % A.group == 0:
                        n = it * A.G + g - len(A.outs) + 1
                        wait(dve, a_ot, n, A.tb if not isinstance(n, int) or n > 0 else 0)
                    W(a_o, u + 1, A.ub)
                    dve.reciprocal(ri[:, c], rs[:, c])
                    dve.drain()
                    dve.tensor_scalar(A.outs[g % len(A.outs)][:, i, out_cols(s)], pb[6 + u % 2][:, 0:A.dv], ri[:, c],
                                      None, ALU.mult).then_inc(a_oe, 1)

                def finish(g):
                    n = it * A.G + g
                    if A.name != "dsa":
                        yb = {"fox": "foxo", "mla": "mlao"}[A.name]
                        dve.wait_ge(yh_done, n + (YH[yb] + 1))
                        dve.tensor_tensor(tile_of(yl, n), pb[5][:, :], tile_of(yh, n).bitcast(F32), ALU.subtract)\
                            .then_inc(a_of, 1)

                if isinstance(it, int) and it == 0:
                    logits(0)
                    logits(1)
                for u in range(A.U):
                    if A.name == "fox" and more and u in (3, 5):
                        crow_dve(dve, it * 2 + (2 + (u == 5)))
                    if u + 2 < A.U:
                        logits(u + 2)
                    if u >= 1:
                        scaled(u - 1)
                    fill_post(dve, split_lo, A, it, u, post, 1)
                fill_post(dve, split_lo, A, it, A.U, post, 1)
                if more:
                    logits(0, it + 1)
                scaled(A.U - 1)
                if more:
                    logits(1, it + 1)
                finish(A.G - 1)
                if extra and isinstance(it, int) and it == 0:
                    extra()
            heads_loop(dve, A, body)

        def stage_act(act, A, it, pairs):
            if A.name == "dsa":
                act.wait_ge(out_free, BASE["dqs"] + 8)
            else:
                act.wait_ge(out_free, it * 2 + (BASE[A.seg] + 2))
            v = it * A.U
            wait(act, a_s, v, A.ub if not isinstance(v, int) or v > 0 else 0)
            for dst, src in pairs:
                act.activation(dst, src, ACT.Copy).then_inc(a_st, 1)

        PR = [diag[:, :], rrow[:, :]]
        dstage = [take(17408, T), take(17920, T), take(19968, T), take(20480, T)]
        lring = [take(18432, T), take(18944, T)]
        DSA = Attention("dsa", 2, 4, P, 128.0 ** -0.5, PR, [ssq[:, :], take(19456, T)],
                        [spare, blk(take(20992, T))], NB, ("gb", 2, 3, 2, (xh, xl, 0)))
        sgb = [take(6144 + j * T, T) for j in range(5)] + [take(15872 + j * T, T) for j in range(3)]
        vX, vXT = take(8192, 8, T), take(12288, NB, D)
        qkX = take(0, 2, T)
        crow = [take(16384, T), take(16896, T)]
        qst, kst = take(17408, T), take(17920, T)
        fdiag = take(19968, T)
        cT = take(20480, NB, 16)
        frow, frow2, frow3 = take(18432, T), take(18944, T), take(19456, T)
        FOX = Attention("fox", 8, 2, 64, 0.125, [take(1024, T), take(1536, T)], [ssq[:, :], take(19456, T)], [spare], 2 * NB,
                        ("fqk", 2, 2, 7, (xh, xl, 0)))
        f_1, f_2, f_3, f_4 = (sem("decay_" + n) for n in "a b c d".split())
        R16 = slice(0, 16)

        def decay_act(act):
            act.wait_ge(f_1, 1)
            act.activation(frow2[R16, :], frow[R16, :], ACT.Abs)
            act.drain()
            act.activation(frow2[R16, :], frow2[R16, :], ACT.Exp, scale=-1.0).then_inc(f_2, 1)
            act.wait_ge(f_1, 2)
            act.activation(frow2[R16, :], frow2[R16, :], ACT.Ln).then_inc(f_2, 1)

        def decay_dve(dve):
            dve.wait_ge(out_free, BASE["ff"] + 1)
            dve.tensor_scalar(frow[R16, :], frow[R16, :], V("foxb", 0, R16), None, ALU.add).then_inc(f_1, 1)
            dve.memset(frow3[R16, :], 1.0)
            dve.wait_ge(f_2, 1)
            dve.tensor_scalar(frow2[R16, :], frow2[R16, :], 1.0, None, ALU.add).then_inc(f_1, 1)
            dve.tensor_scalar(frow[R16, :], frow[R16, :], 0.0, None, ALU.min)
            dve.wait_ge(f_2, 2)
            dve.drain()
            dve.tensor_tensor(frow2[R16, :], frow[R16, :], frow2[R16, :], ALU.subtract)
            dve.drain()
            dve.tensor_tensor_scan(frow[R16, :], frow3[R16, :], frow2[R16, :], 0.0, ALU.mult, ALU.add).then_inc(f_3, 1)
            dve.wait_ge(f_4, 1)
            dve.tensor_copy(cT, blk(pb[6][:, :])[:, :, 0:16])
            dve.drain()

        def decay_pe(pe):
            pe.wait_ge(f_3, 1)
            for b in range(NB):
                m = pe.transpose(pb[6][:, B(b)], frow[:, B(b)], ident)
            m.then_inc(f_4, 1)

        kM, qM, vMT = take(0, 16, T), take(8192, 2, T), take(16384, NB, D)
        cqr, vM, ckr = take(8192, 6, T), take(11264, 8, T), take(16384, 2, T)
        rck = take(17408, T)
        cs, rt = take(20480, T), take(20992, T)
        ang, kf, ri32 = take(8192, T), take(8704, T), take(9216, T).bitcast(I32)
        posi = take(9728, T).bitcast(I32)
        MLA = Attention("mla", 8, 2, 64, 96.0 ** -0.5, PR, [ssq[:, :], take(15360, T)], [spare], 2 * NB,
                        ("uq", 2, 2, 7, (xh, xl, 2)))
        mst = [take(20992, T), mats[:, MO["lastrow"]:MO["maskT"] + 1, :].rearrange("p a b -> p (a b)")]
        r_ang, r_cs, r_rt, r_kr, r_k0, r_kall = (
            sem("mla_" + n) for n in "angles sines k_turned k_rope k_rope0 k_rope_all".split())
        LO, HI64 = slice(0, 64), slice(64, 128)

        def rope_dve(dve):
            dve.wait_ge(s_pos, 16)
            dve.tensor_copy(ang, posi)
            dve.drain()
            dve.tensor_scalar(ang, ang, V("freq"), None, ALU.mult)
            dve.drain()
            dve.tensor_scalar(ri32, ang, 1.0 / (2.0 * np.pi), None, ALU.mult)
            dve.drain()
            dve.tensor_copy(kf, ri32)
            dve.drain()
            for part in (TWO_PI_HI, TWO_PI_LO):
                dve.scalar_tensor_tensor(out=ang, in0=kf, scalar=-part, in1=ang, op0=ALU.mult, op1=ALU.add)
                dve.drain()
            dve.tensor_scalar(ang, ang, V("phase"), None, ALU.add)
            dve.drain()
            dve.tensor_scalar(kf, ang, float(np.pi), -2.0 * np.pi, ALU.is_gt, ALU.mult)
            dve.drain()
            dve.tensor_tensor(ang, ang, kf, ALU.add)
            dve.drain()
            dve.tensor_scalar(ang, ang, PI_F, -PI_F, ALU.min, ALU.max).then_inc(r_ang, 1)

        GEMMS = [n for n, _, _ in SEGS]

        @block.sync
        def _(sp):
            for t in range(DT):
                sp.dma_start(h[:, t, :], I["x"][t]).then_inc(s_xt[t], 16)
            sp.dma_start(vec[:, :], I["vec"]).then_inc(s_const, 16)
            sp.dma_start(mats[:, 0:2, :], I["mats"][:, 0:2, :]).then_inc(s_const, 16)

            def other_mats():
                sp.dma_start(mats[:, 2:, :], I["mats"][:, 2:, :]).then_inc(s_mats, 16)
            for seg in GEMMS:
                load(sp, seg, {1: other_mats} if seg == "gq" else None)
            for t in range(DT):
                sp.wait_ge(n_tmp, NTMP["final2"] + t + 1)
                sp.dma_start(out[t], h[:, t, :]).then_inc(s_out, 16)
            sp.wait_ge(s_out, 16 * DT)

        @block.gpsimd
        def _(pool):
            pool.memset(mhalf[:, :], -0.5).then_inc(s_set, 1)
            pool.wait_ge(s_set, 1)
            late_pool(pool, "norm1")
            gdn_pool(pool)
            index_pool(pool)
            pool.wait_ge(w_lo, BASE["dqs"] + 2)
            split_and(pool, split_lo, "dqs", None)
            split_first(pool, split_lo, "gb", None)

            for t in range(8):
                pool.wait_ge(yh_done, t + 1)
                pool.tensor_tensor(yl[:, t, :], sgb[t], yh[:, t, :].bitcast(F32), ALU.subtract).then_inc(y_ready, 1)
            sum_squares(pool, "wout", 8)
            late_pool(pool, "norm2")
            for ch in range(3):
                hidden_pool(pool, "c", ch)
            for t in range(8):
                m = SQ["c2dn"] + 2 * t
                for k, total in ((0, ssq[:, :]), (1, ssq2)):
                    pool.wait_ge(sq_done, m + k + 1)
                    if t == 0:
                        wait(pool, n_ms, NROW["final1"])
                        pool.tensor_copy(total, sqb[:, k, :]).then_inc(ssq_done, 1)
                    else:
                        pool.wait_ge(ssq_done, m + k - 1)
                        pool.tensor_tensor(total, total, sqb[:, k, :], ALU.add).then_inc(ssq_done, 1)
            for k, name in enumerate(("final1", "an0")):
                pool.wait_ge(n_ev, NROW[name] + 1)
                r_ = row2[:, k * NB:(k + 1) * NB]
                pool.tensor_tensor(r_, r_, mhalf[:, 0:NB], ALU.pow).then_inc(n_pw, 1)
            sum_squares(pool, "fo", 8)
            late_pool(pool, "fn0")
            for ch in range(3):
                hidden_pool(pool, "s", ch)
            sum_squares(pool, "s2dn", 8)
            late_pool(pool, "kvn")
            sum_squares(pool, "ckvsq", 2)
            late_pool(pool, "ckvn")
            sum_squares(pool, "cqsq", 6)
            late_pool(pool, "cqn")
            pool.wait_ge(n_pw, NROW["cqn"] + 1)
            pool.wait_ge(r_k0, 1)
            for q in range(1, 16):
                pool.tensor_copy(kM[HI64, q, :], kM[HI64, 0, :]).then_inc(r_kall, 1)
            pool.wait_ge(r_kall, 15)
            sum_squares(pool, "mo", 8)
            late_pool(pool, "fn1")
            for ch in range(3):
                hidden_pool(pool, "m", ch)
            sum_squares(pool, "m2dn", 8)
            norm_pool(pool, "final2")

        @block.scalar
        def _(act):
            for t in range(DT):
                act.wait_ge(s_xt[t], 16)
                act.activation(kF[:, t, :], h[:, t, :], ACT.Square).then_inc(first_sq, 1)
            split_hi(act, 0, 0, 0, KT_OF[0])
            norm_act(act, "norm1")
            split_hi(act, 1, 0, 1, KT_OF[1])
            act.wait_ge(s_mats, 16)
            act.activation(identb[:, :], ident, ACT.Copy).then_inc(s_maskb, 1)
            act.activation(maskTb[:, :], M("maskT"), ACT.Copy).then_inc(s_maskb, 1)
            act.activation(maskSb[:, :], M("maskS"), ACT.Copy).then_inc(s_maskb, 1)
            gconv_act(act, "gq", h)
            gconv_act(act, "gk", kF)

            def misc_post(n, t, q, r, bank):
                act.wait_ge(mm_done, n + 1)
                act.activation(misc, bank[:, :], ACT.Copy).then_inc(out_free, 1)
            split_and(act, split_hi, "misc", misc_post)
            act.drain()
            gmisc_act(act)
            gconv_act(act, "gv", vF)
            gexps_act(act)
            gdn_act(act)
            split_and(act, split_hi, "idx", copy_out(act, DS, 12))
            index_act(act)
            split_and(act, split_hi, "dqs", copy_out(act, DS))

            def gb_post(n, t, q, r, bank):
                act.wait_ge(mm_done, n + 1)
                act.activation(sgb[t], bank[:, :], ACT.Sigmoid, bias=V("gbb", t)).then_inc(out_free, 1)

            def mix_hi(q):
                for t in (2 * q, 2 * q + 1):
                    act.wait_ge(gate_mul, t + 1)
                    act.activation(yh[:, t, :], sgb[t], ACT.Copy).then_inc(yh_done, 1)
            split_first(act, split_hi, "gb", gb_post)
            v_copy(act, 0, 2, vD, 0)
            attn_act(act, DSA, lambda n: tile_of(oD, n), gb_post,
                     lambda it: [(dstage[s], DS[:, it * 4 + s, :]) for s in range(4)], lambda: (mix_hi(0), mix_hi(1)))
            for q in (2, 3):
                mix_hi(q)
            act.wait_ge(gate_mul, 8)
            act.dma_start(h[:, :, :], I["x"].rearrange("t p n -> p t n")).then_inc(s_x2, 16)
            split_and(act, split_hi, "wout", square_h(act, "wout", "norm2"))
            act.wait_ge(s_gain, 1)
            for ch in range(3):
                hidden_act(act, "c", ch)
                split_and(act, split_hi, f"c{ch}dn",
                          square_h(act, "c2dn", "an0", "an0f", "final1") if ch == 2 else None)
            split_and(act, split_hi, "fv", None)
            split_and(act, split_hi, "ff", None)
            decay_act(act)
            split_first(act, split_hi, "fqk", None)
            v_copy(act, 0, 8, vXT, 2)
            crow_act(act, 0, 0)
            crow_act(act, 1, 1)
            attn_act(act, FOX, lambda n: tile_of(yh, n), None,
                     lambda it: [(qst, qkX[:, 0, :]), (kst, qkX[:, 1, :])])
            split_and(act, split_hi, "fo", square_h(act, "fo", "fn0"))
            act.dma_start(posi, I["pos"].broadcast_to([P, T])).then_inc(s_pos, 16)
            for ch in range(3):
                hidden_act(act, "s", ch)
                split_and(act, split_hi, f"s{ch}dn", square_h(act, "s2dn", "kvn") if ch == 2 else None)
                if ch == 0:
                    act.wait_ge(r_ang, 1)
                    act.activation(cs, ang, ACT.Sin).then_inc(r_cs, 1)

            def kva_post(n, t, q, r, bank):
                if t == 0:
                    act.wait_ge(mm_done, BASE["kva"])
                    for k in range(DT):
                        late_hi(act, "an1", k, h[:, k, :])
                act.wait_ge(out_free, n + 1)
                if t < 2:
                    act.wait_ge(mm_done, BASE["kva"] + 3)
                    late_hi(act, "ckvn", t, ckr[:, t, :])
                    square(act, "ckvsq", t, t, ckr[:, t, :])
            split_and(act, split_hi, "kva", None)
            for t in range(3):
                kva_post(BASE["kva"] + t, t, 0, t, None)
            act.wait_ge(r_kr, 1)
            act.activation(kM[HI64, 0, :], pb[2][HI64, :], ACT.Copy).then_inc(r_k0, 1)

            def dq_post(n, t, q, r, bank):
                act.wait_ge(out_free, n + 1)
                late_hi(act, "cqn", t, cqr[:, t, :])
                square(act, "cqsq", t, r, cqr[:, t, :])
            split_and(act, split_hi, "dq", dq_post)
            split_and(act, split_hi, "uk", None)
            split_and(act, split_hi, "uv", None)
            split_first(act, split_hi, "uq", None)
            v_copy(act, 0, 8, vMT, 10)
            attn_act(act, MLA, lambda n: tile_of(yh, n), None, lambda it: [(mst[s], qM[:, s, :]) for s in range(2)])
            split_and(act, split_hi, "mo", square_h(act, "mo", "fn1"))
            for ch in range(3):
                hidden_act(act, "m", ch)
                split_and(act, split_hi, f"m{ch}dn", square_h(act, "m2dn") if ch == 2 else None)

        @block.vector
        def _(dve):
            for t in range(DT):
                dve.wait_ge(first_sq, t + 1)
                if t == 0:
                    dve.tensor_copy(ssq[:, :], kF[:, 0, :]).then_inc(first_sum, 1)
                else:
                    dve.wait_ge(first_sum, t)
                    dve.tensor_tensor(ssq[:, :], ssq[:, :], kF[:, t, :], ALU.add).then_inc(first_sum, 1)
            dve.wait_ge(s_const, 32)
            late_diag(dve, "norm1", D)
            split_lo(dve, 0, 0, 0, KT_OF[0])
            late_row(dve, "norm1", rrow[:, :])
            for t in range(DT + 1):
                if t < DT:
                    if t >= 2:
                        dve.wait_ge(x_ready, t - 1)
                    dve.scalar_tensor_tensor(out=tmpb[:, t % 2, :], in0=h[:, t, :], scalar=V("norm1", t), in1=rrow[:, :],
                                             op0=ALU.mult, op1=ALU.mult).then_inc(n_tmp, 1)
                if t >= 1:
                    dve.wait_ge(n_hi, t)
                    dve.tensor_tensor(xl[:, t - 1, :], tmpb[:, (t - 1) % 2, :], xh[:, t - 1, :].bitcast(F32),
                                      ALU.subtract).then_inc(x_ready, 1)
            split_lo(dve, 1, 0, 1, KT_OF[1])
            dve.wait_ge(s_mats, 16)
            gconv_dve(dve, "gq", h, 0)
            gconv_dve(dve, "gk", kF, 8)
            split_and(dve, split_lo, "misc", None)
            gmisc_dve(dve)
            gconv_dve(dve, "gv", vF, 16, {1: gcols_dve, 6: glast_dve})
            gdn_dve(dve)
            gate_dve(dve, GH - 2, GH)
            split_and(dve, split_lo, "idx", None)
            index_dve(dve)
            v_copy(dve, 1, 2, vD, 0)
            dve.wait_ge(w_lo, BASE["gb"] + 4)

            def mix(q):
                dve.wait_ge(a_of, 2 * q + 2)
                dve.wait_ge(out_free, BASE["gb"] + 2 * q + 2)
                for t in (2 * q, 2 * q + 1):
                    dve.tensor_tensor(sgb[t], sgb[t], oD[:, t, :], ALU.mult)
                dve.drain()
                for t in (2 * q, 2 * q + 1):
                    dve.tensor_tensor(sgb[t], sgb[t], h[:, t, :], ALU.add).then_inc(gate_mul, 1)
            attn_dve(dve, DSA, lambda s: slice(0, P), None, lambda: (mix(0), mix(1)))
            for q in (2, 3):
                mix(q)
            dve.wait_ge(s_x2, 16)
            split_and(dve, split_lo, "wout", add_to_h(dve, "norm2"), True)
            late_diag(dve, "norm2", D)
            dve.tensor_tensor(vec[:, VO["an0f"]:VO["an0f"] + DT], vec[:, VO["an0"]:VO["an0"] + DT],
                              vec[:, VO["final1"]:VO["final1"] + DT], ALU.mult).then_inc(s_gain, 1)
            for ch in range(3):
                hidden_dve(dve, "c", ch, "norm2" if ch == 0 else None)
                split_and(dve, split_lo, f"c{ch}dn", add_to_h(dve, "an0", "an0f") if ch == 2 else add_to_h(dve), True)
            ra_, rb2 = row2[:, 0:NB], row2[:, NB:2 * NB]
            dve.wait_ge(n_ms, NROW["final1"] + 2)
            dve.tensor_scalar(ra_, pb[7][:, 0:NB], 1.0 / D, EPS, ALU.mult, ALU.add).then_inc(n_ev, 1)
            dve.wait_ge(n_pw, NROW["final1"] + 1)
            dve.tensor_tensor(rb2, ra_, ra_, ALU.mult)
            dve.drain()
            dve.tensor_tensor(rb2, rb2, pb[7][:, NB:2 * NB], ALU.mult)
            dve.drain()
            dve.tensor_scalar(rb2, rb2, 1.0 / D, EPS, ALU.mult, ALU.add).then_inc(n_ev, 1)
            dve.wait_ge(n_pw, NROW["an0"] + 1)
            dve.tensor_tensor(rb2, ra_, rb2, ALU.mult)
            dve.drain()
            dve.tensor_tensor(blk(diag[:, :]), rep(ident, NB), bc(rb2, P), ALU.mult).then_inc(n_dg, 1)

            def fv_post(n, t, q, r, bank):
                if isinstance(t, int) and t == 0:
                    late_row(dve, "final1", rrow[:, :])
                    dve.tensor_tensor(blk(diag[:, :]), rep(ident, NB), bc(ra_, P), ALU.mult).then_inc(n_dg, 1)
                scale_out(dve, vX)(n, t, q, r, bank)
                if not isinstance(t, int) or t >= 2:
                    final_h(t - 2)

            def final_h(t):
                dve.scalar_tensor_tensor(out=tile_of(h, t), in0=tile_of(h, t), scalar=V("final1", t),
                                         in1=pb[7][:, :], op0=ALU.mult, op1=ALU.mult)

            def fv_step(n, t, q, r, bank):
                if isinstance(t, int) and t == 2:
                    pass
                fv_post(n, t, q, r, bank)
                if isinstance(t, int) and t == 1:
                    dve.wait_ge(n_row, NROW["final1"] + 2)
            split_and(dve, split_lo, "fv", fv_step)
            final_h(6)
            final_h(7)

            def ff_post(n, t, q, r, bank):
                dve.wait_ge(mm_done, n + 1)
                dve.tensor_tensor(frow, bank[:, :], rrow[:, :], ALU.mult).then_inc(out_free, 1)
            split_and(dve, split_lo, "ff", ff_post)
            decay_dve(dve)

            def fqk_post(n, t, q, r, bank):
                if not isinstance(t, int) or t >= 2:
                    dve.wait_ge(a_st, q * 2 + (FOX.sb_ + 2))
                dve.wait_ge(mm_done, n + 1)
                dve.tensor_tensor(qkX[:, r, :], bank[:, :], rrow[:, :], ALU.mult).then_inc(out_free, 1)
            split_first(dve, split_lo, "fqk", fqk_post)
            v_copy(dve, 1, 8, vXT, 2)
            crow_dve(dve, 0)
            crow_dve(dve, 1)
            attn_dve(dve, FOX, lambda s: slice(64 * s, 64 * s + 64), fqk_post)
            split_and(dve, split_lo, "fo", add_to_h(dve, "fn0"), True)
            late_diag(dve, "fn0", D)
            for ch in range(3):
                hidden_dve(dve, "s", ch, "fn0" if ch == 0 else None)
                split_and(dve, split_lo, f"s{ch}dn", add_to_h(dve, "kvn") if ch == 2 else add_to_h(dve), True)
                if ch == 0:
                    rope_dve(dve)
            late_diag(dve, "kvn", D)

            def kva_post(n, t, q, r, bank):
                if t == 0:
                    late_row(dve, "kvn", rrow[:, :])
                    dve.wait_ge(r_cs, 1)
                    dve.tensor_tensor(rt, cs, rrow[:, :], ALU.mult)
                    dve.wait_ge(out_free, n)
                dve.wait_ge(mm_done, n + 1)
                if t < 2:
                    dve.tensor_tensor(ckr[:, t, :], bank[:, :], rrow[:, :], ALU.mult).then_inc(out_free, 1)
                else:
                    dve.drain()
                    dve.tensor_tensor(rt, bank[:, :], rt, ALU.mult).then_inc(out_free, 1)
            split_and(dve, split_lo, "kva", kva_post)
            for t in range(DT):
                late_lo(dve, "an1", t, h[:, t, :])
            for t in range(2):
                late_lo(dve, "ckvn", t, ckr[:, t, :])

            def dq_post(n, t, q, r, bank):
                if t == 2:
                    late_diag(dve, "ckvn", 256)
                if t == 3:
                    late_row(dve, "ckvn", rck)
                if t >= 1:
                    late_lo(dve, "cqn", t - 1, cqr[:, t - 1, :])
                scale_out(dve, cqr)(n, t, q, r, bank)
            split_and(dve, split_lo, "dq", dq_post)
            late_lo(dve, "cqn", 5, cqr[:, 5, :])

            def uk_post(n, t, q, r, bank):
                dve.wait_ge(mm_done, n + 1)
                dve.tensor_tensor(tile_of(kM, t * 2, LO), bank[LO, :], rck[LO, :], ALU.mult)
                dve.tensor_tensor(tile_of(kM, t * 2 + 1, LO), bank[HI64, :], rck[HI64, :], ALU.mult).then_inc(out_free, 1)
                if isinstance(t, int) and t == 1:
                    late_diag(dve, "cqn", 768)
            split_and(dve, split_lo, "uk", uk_post)

            def uv_post(n, t, q, r, bank):
                dve.wait_ge(mm_done, n + 1)
                dve.tensor_tensor(tile_of(vM, t), bank[:, :], rck, ALU.mult).then_inc(out_free, 1)
            split_and(dve, split_lo, "uv", uv_post)
            dve.wait_ge(n_row, NROW["cqn"] + 1)
            dve.tensor_tensor(cs[HI64, :], cs[HI64, :], pb[6][HI64, :], ALU.mult)
            dve.tensor_copy(cs[LO, :], pb[6][LO, :])
            dve.drain()

            def uq_post(n, t, q, r, bank):
                if not isinstance(t, int) or t >= 2:
                    dve.wait_ge(a_st, q * 2 + (MLA.sb_ + 2))
                dve.wait_ge(mm_done, n + 1)
                dve.tensor_tensor(qM[:, r, :], bank[:, :], cs, ALU.mult).then_inc(out_free, 1)
            split_first(dve, split_lo, "uq", uq_post)
            v_copy(dve, 1, 8, vMT, 10)
            attn_dve(dve, MLA, lambda s: slice(64 * s, 64 * s + 64), uq_post)
            split_and(dve, split_lo, "mo", add_to_h(dve, "fn1"), True)
            late_diag(dve, "fn1", D)
            for ch in range(3):
                hidden_dve(dve, "m", ch, "fn1" if ch == 0 else None)
                split_and(dve, split_lo, f"m{ch}dn", add_to_h(dve), True)
            norm_dve(dve, "final2", h, D, "final2")

        @block.tensor
        def _(pe):
            pe.wait_ge(s_const, 32)
            pe.wait_ge(first_sum, DT)
            for b in range(NB):
                m = pe.matmul(pb[7][:, b:b + 1], ssq[:, B(b)], ones[:, 0:1], start=True, stop=True)
            m.then_inc(n_ms, 1)
            norm_pe_row(pe, "norm1")
            products(pe, "gq", xh, xl, ready=(x_ready, XR["norm1"]))
            products(pe, "gk", xh, xl)
            products(pe, "misc", xh, xl)
            products(pe, "gv", xh, xl, between={(0, 7): lambda: gmisc_pe(pe), (6, 3): lambda: glast_pe(pe)})
            gdn_pe(pe)
            pe.wait_ge(g_of, GH)
            products(pe, "idx", xh, xl)
            index_pe(pe)
            products(pe, "dqs", xh, xl)
            products_first(pe, "gb", xh, xl)
            pe.wait_ge(i_r, len(SCORES))
            v_pe(pe, [DS[:, 10, :], DS[:, 11, :]], 0)
            pe.wait_ge(v_ea, 1)
            pe.wait_ge(v_ed, 1)
            pe.wait_ge(i_mask, NB - 1)
            attn_pe(pe, DSA, lambda s, i: dstage[s][:, B(i)],
                    lambda it, s, nk: tile_of(DS, it + 8)[:, 0:nk],
                    lambda it, s, j: vD[:, j, bass.ds(it * P, P)] if not isinstance(it, int) else vD[:, j, B(it)], 4)
            products(pe, "wout", yh, yl, ready=(y_ready, YR["gb"]))
            for ch in range(3):
                products(pe, f"c{ch}up", xh, xl, ready=(x_ready, XR["norm2"]), between=late_pe(pe, "norm2") if ch == 0 else None)
                products(pe, f"c{ch}dn", yh, yl, ready=(y_ready, YR["c"] + PAIRS[ch][0]))

            def two_sums():
                pe.wait_ge(ssq_done, SQ_END["final1"])
                for k, total in enumerate((ssq[:, :], ssq2)):
                    for b in range(NB):
                        m = pe.matmul(pb[7][:, k * NB + b:k * NB + b + 1], total[:, B(b)], ones[:, 0:1], start=True, stop=True)
                    m.then_inc(n_ms, 1)

            def row_r1():
                pe.wait_ge(n_dg, NROW["final1"] + 2)
                pe.matmul(pb[7][:, :], ones, diag[:, :], start=True, stop=True).then_inc(n_row, 1)
            products(pe, "fv", xh, xl, ready=(x_ready, XR["an0"]),
                     between={(0, 4): two_sums, (1, 1): lambda: norm_pe_row(pe, "final1"), (1, 7): row_r1})
            products(pe, "ff", xh, xl)
            products_first(pe, "fqk", xh, xl)
            decay_pe(pe)
            v_pe(pe, [vX[:, t, :] for t in range(8)], 2)
            pe.wait_ge(v_ea, 5)
            pe.wait_ge(v_ed, 5)
            crow_pe(pe, 0)
            crow_pe(pe, 1)
            pe.wait_ge(a_cr, 2)

            def vcols(buf, it, s, j):
                if isinstance(it, int):
                    return buf[:, j, it * P + 64 * s:it * P + 64 * s + 64]
                return buf[:, j, bass.ds(it * P + 64 * s, 64)]
            attn_pe(pe, FOX, lambda s, i: qst[64 * s:64 * s + 64, B(i)],
                    lambda it, s, nk: kst[64 * s:64 * s + 64, 0:nk],
                    lambda it, s, j: vcols(vXT, it, s, j), 2)
            pe.wait_ge(a_of, 16)
            products(pe, "fo", yh, yl)
            for ch in range(3):
                products(pe, f"s{ch}up", xh, xl, ready=(x_ready, XR["fn0"]), between=late_pe(pe, "fn0") if ch == 0 else None)
                products(pe, f"s{ch}dn", yh, yl, ready=(y_ready, YR["s"] + PAIRS[ch][0]))
            products(pe, "kva", xh, xl, ready=(x_ready, XR["kvn"]), between=late_pe(pe, "kvn"))

            def k_rope():
                pe.wait_ge(out_free, BASE["kva"] + 3)
                pe.matmul(pb[2][:, :], M("ropesel"), rt, start=True, stop=True).then_inc(r_kr, 1)
            products(pe, "dq", yh, yl, ready=(y_ready, YR["an1"]),
                     between={(0, 7): k_rope, (2, 0): lambda: norm_pe(pe, "ckvn", row=False),
                              (3, 3): lambda: norm_pe_row(pe, "ckvn")})
            products(pe, "uk", xh, xl, ready=(x_ready, XR["ckvn"]),
                     between={(1, 1): lambda: norm_pe(pe, "cqn", row=False), (6, 1): lambda: norm_pe_row(pe, "cqn")})
            products(pe, "uv", xh, xl)
            products_first(pe, "uq", xh, xl, tile0=2, ready=(x_ready, XR["cqn"]))
            v_pe(pe, [vM[:, t, :] for t in range(8)], 10)
            pe.wait_ge(v_ea, 9)
            pe.wait_ge(v_ed, 9)
            pe.wait_ge(r_kall, 15)
            attn_pe(pe, MLA, lambda s, i: mst[s][:, B(i)],
                    lambda it, s, nk: tile_of(kM, it * 2 + s)[:, 0:nk],
                    lambda it, s, j: vcols(vMT, it, s, j), 2)
            pe.wait_ge(a_of, 24)
            products(pe, "mo", yh, yl)
            for ch in range(3):
                products(pe, f"m{ch}up", xh, xl, ready=(x_ready, XR["fn1"]), between=late_pe(pe, "fn1") if ch == 0 else None)
                products(pe, f"m{ch}dn", yh, yl, ready=(y_ready, YR["m"] + PAIRS[ch][0]))
            norm_pe(pe, "final2")


def _panels(w):
    k, n = w.shape
    return np.ascontiguousarray(w.reshape(k // P, P, n // P, P).transpose(2, 1, 0, 3)).reshape(n // P, P, -1)


def _columns(v):
    return v.reshape(-1, P).T


def _spread(parts, n=P):
    rows = parts[0][1].shape[0]
    block = np.zeros((rows, n), np.float32)
    for off, a in parts:
        block[:, off:off + a.shape[1]] = a
    return block


def _matrices():
    i, j = np.arange(P)[:, None], np.arange(P)[None, :]
    out = np.zeros((P, len(MATS), P), np.float32)
    out[:, MO["ident"]] = i == j
    out[:, MO["ones"]] = 1.0
    out[:, MO["lastrow"]] = (i == P - 1) * np.ones_like(j)
    out[:, MO["blk64"]] = (i // 64 == j // 64) / 64.0
    r = (j - 64) % 32
    out[:, MO["ropesel"]] = (j >= 64) & ((i == r) | (i == 32 + r))
    out[:, MO["maskT"]] = np.where(j < i, NEG, 0.0)
    out[:, MO["maskS"]] = np.where(j > i, NEG, 0.0)
    for l in range(LEVELS):
        b = 1 << l
        out[:, MO[f"lev{l}"]] = (i // (2 * b) == j // (2 * b)) & (i // b % 2 == 0) & (j // b % 2 == 1)
    return out


def _interleave(w, first, cnt):
    cols = [w[:, side * FF + t * P:side * FF + t * P + P] for t in range(first, first + cnt) for side in (0, 1)]
    return np.concatenate(cols, axis=1)


def _layout(a):
    w = a["w_in"][0]
    o = np.cumsum([0, 3072, 1024, 8, 8, 1024, 256, 256, 512, 64, 8, 1024, 1024])
    qkv, z, ga_, gb_, dq, dk, dv, iq, ik, iw, gate_a, gate_b = (w[:, o[n]:o[n + 1]] for n in range(12))
    r = {"gq": qkv[:, 0:1024], "gk": qkv[:, 1024:2048], "gv": qkv[:, 2048:3072],
         "misc": _spread([(0, ga_), (32, gb_), (64, iw)]), "zga": np.stack([z.reshape(D, DT, P), gate_a.reshape(D, DT, P)], axis=2).reshape(D, 2048),
         "idx": np.concatenate([iq, ik, ik], axis=1), "dkv": np.concatenate([dk, dv], axis=1), "dqs": dq, "gb": gate_b, "wout": a["w_out"][0]}
    up, dn = a["ffn_w_up"][0], a["ffn_w_down"][0]
    for l, u, d in (("c", up, dn),) + tuple(
            (l, np.concatenate([a["w_gate_2"][k], a["w_up_2"][k]], axis=1), a["w_down_2"][k])
            for k, l in ((0, "s"), (1, "m"))):
        for ch, (first, cnt) in enumerate(PAIRS):
            r[f"{l}{ch}up"] = _interleave(u, first, cnt)
            r[f"{l}{ch}dn"] = d[first * P:(first + cnt) * P]
    f = a["fox_w_in_2"][0]
    r.update(fqk=f[:, 0:2048].reshape(D, 2, DT, P).transpose(0, 2, 1, 3).reshape(D, 2048), fv=f[:, 2048:3072], ff=_spread([(0, f[:, 3072:])]),
             fo=a["fox_w_o_2"][0])
    kv = a["w_kv_a_2"]
    rope = kv[:, 256:288]
    turn = np.concatenate([rope, rope[:, 16:32], rope[:, 0:16]], axis=1)
    r["kva"] = np.concatenate([kv[:, 0:256], turn, turn], axis=1)
    r["uk"], r["uv"] = a["w_uk_2"].reshape(256, 1024), a["w_uv_2"].reshape(256, 1024)
    r["dq"] = a["mla_w_dq_2"][0]
    uq = a["mla_w_uq_2"][0].reshape(768, 16, 96)
    r["uq"] = np.concatenate([uq, uq[:, :, 80:96], uq[:, :, 64:80]], axis=2).reshape(768, 2048)
    r["mo"] = a["mla_w_o_2"][0]
    out = {n: _panels(np.ascontiguousarray(v)) for n, v in r.items()}
    vec = np.zeros((P, NV), np.float32)

    def put(name, cols):
        vec[0:cols.shape[0], VO[name]:VO[name] + cols.shape[1]] = cols
    for name, v in (("norm1", a["norm1_g"][0]), ("norm2", a["norm2_g"][0]), ("final1", a["final_g"]),
                    ("an0", a["attn_norm_2"][0]), ("an1", a["attn_norm_2"][1]), ("fn0", a["ffn_norm_2"][0]),
                    ("fn1", a["ffn_norm_2"][1]), ("kvn", a["kv_norm_2"]), ("final2", a["final_norm_2"]),
                    ("ckvn", a["ckv_norm_2"]), ("cqn", a["cq_norm_2"][0]), ("gdng", a["gdn_norm_g"][0]),
                    ("gba", a["branch_gate_b"][0, 0:1024]), ("gbb", a["branch_gate_b"][0, 1024:2048]),
                    ("fbias", a["ffn_conv_b"][0])):
        put(name, _columns(v))
    put("gconv", a["gdn_conv_w"][0].reshape(4, 24, P).transpose(2, 1, 0).reshape(P, 96))
    put("fconv", a["ffn_conv_w"][0].reshape(3, 44, P).transpose(2, 1, 0).reshape(P, 132))
    put("ikg", np.concatenate([a["idx_k_norm_g"][0]] * 2)[:, None])
    put("alog", a["gdn_a_log"][0][:, None])
    put("dtb", a["gdn_dt_bias"][0][:, None])
    put("foxb", a["fox_b_f_2"][0][:, None])
    row = np.arange(P)
    put("freq", (10000.0 ** (-(row % 16) * 2.0 / 32)).astype(np.float32)[:, None])
    sine = row // 32 % 2 == 1
    put("phase", np.where(sine, np.where(row % 32 < 16, np.pi, 0.0), np.pi / 2).astype(np.float32)[:, None])
    out["vec"] = vec
    out["mats"] = _matrices()
    out["x"] = np.ascontiguousarray(a["x"][0].T).reshape(DT, P, T)
    out["pos"] = np.ascontiguousarray(a["positions_2"]).astype(np.int32)
    return out


def kernel(**inputs):
    import concourse.bacc as _bacc
    from concourse.bass_utils import run_bass_kernel_spmd as _run

    arrays = _layout({k: np.asarray(v) for k, v in inputs.items()})
    nc = _bacc.Bacc("TRN2", target_bir_lowering=False, num_devices=1)
    arrays = {f"in_{k}": v for k, v in arrays.items()}
    ins = {k[3:]: nc.dram_tensor(k, v.shape, mybir.dt.from_np(v.dtype), kind="ExternalInput").ap()
           for k, v in arrays.items()}
    out = nc.dram_tensor("out_y", (DT, P, T), F32, kind="ExternalOutput").ap()
    build(nc, ins, out)
    r = _run(nc, [arrays], core_ids=[0])
    y = r.results[0]["out_y"]
    return np.ascontiguousarray(y.reshape(D, T).T).reshape(1, T, D)
```
